# Optimizing a Trainium2 kernel written in Bass

```python
import jax, jax.numpy as jnp
from jax import lax
import numpy as np

D_MODEL = 1024
BATCH = 1
SEQ = 1024
DEPTH = 1

CHUNK = 64
RMS_EPS = 1e-6
N_MOD = 6

HG_HEADS = 4
HG_DK = 128
HG_DV = 128
HG_WIDTH = HG_HEADS * HG_DV

SW_HEADS = 8
SW_KV_HEADS = 2
SW_HEAD_DIM = 64
SW_GROUP = SW_HEADS // SW_KV_HEADS
SW_WIDTH = SW_HEADS * SW_HEAD_DIM
WINDOW = 128
WINDOW_CHUNKS = WINDOW // CHUNK

N_BRANCH = 2
BRANCH_WIDTH = 512

SPLIT_SIZES = (
    HG_HEADS * HG_DK,
    HG_HEADS * HG_DK,
    HG_HEADS * HG_DV,
    HG_WIDTH,
    SW_WIDTH,
    SW_KV_HEADS * SW_HEAD_DIM,
    SW_KV_HEADS * SW_HEAD_DIM,
    N_BRANCH * D_MODEL,
)
D_IN = sum(SPLIT_SIZES)

PEER_HEADS = 8
N_KEYS = 128
N_EXPERTS = N_KEYS * N_KEYS
PEER_DQ = 256
PEER_TOPK = 16
PEER_BLOCK = 128

kernel_name = "chunk_causal_hybrid_hgrn2_swa_peer"

def rms_norm(x, w):
    xf = x.astype(jnp.float32)
    y = xf * lax.rsqrt(jnp.mean(xf * xf, axis=-1, keepdims=True) + RMS_EPS)
    return (y * w.astype(jnp.float32)).astype(x.dtype)

def hgrn2_mix(q, f_logit, i, g, lb, norm_w):
    B, S, _ = q.shape
    n_chunks = S // CHUNK
    dt = q.dtype
    f32 = jnp.float32
    lb = lb.astype(f32)
    f = lb + (1.0 - lb) * jax.nn.sigmoid(f_logit.astype(f32))
    log_f = jnp.log(f)
    k = 1.0 - f

    def to_chunks(t, d):
        return t.reshape(B, n_chunks, CHUNK, HG_HEADS, d).transpose(1, 0, 3, 2, 4)

    qc = to_chunks(q.astype(f32), HG_DK)
    kc = to_chunks(k, HG_DK)
    vc = to_chunks(i.astype(f32), HG_DV)
    lfc = to_chunks(log_f, HG_DK)
    causal = jnp.tril(jnp.ones((CHUNK, CHUNK), dtype=bool))

    def step(state, inp):
        q_, k_, v_, lf = inp
        b = jnp.cumsum(lf, axis=-2)
        diff = b[:, :, :, None, :] - b[:, :, None, :, :]
        decay = jnp.exp(jnp.where(causal[:, :, None], diff, -jnp.inf))
        scores = jnp.einsum('bhtd,bhsd,bhtsd->bhts', q_, k_, decay)
        o = (jnp.einsum('bhts,bhsv->bhtv', scores, v_)
             + jnp.einsum('bhtd,bhdv->bhtv', q_ * jnp.exp(b), state))
        b_last = b[:, :, -1, :]
        state = (jnp.exp(b_last)[..., None] * state
                 + jnp.einsum('bhsd,bhsv->bhdv', k_ * jnp.exp(b_last[:, :, None, :] - b), v_))
        return state, o

    state0 = jnp.zeros((B, HG_HEADS, HG_DK, HG_DV), f32)
    _, o = lax.scan(step, state0, (qc, kc, vc, lfc))
    o = o.transpose(1, 0, 3, 2, 4).reshape(B, S, HG_HEADS, HG_DV)
    o = rms_norm(o, norm_w)
    o = o * jax.nn.silu(g.astype(f32).reshape(B, S, HG_HEADS, HG_DV))
    return o.reshape(B, S, HG_WIDTH).astype(dt)

def swa_sink_mix(q, k, v, q_norm_w, k_norm_w, sinks):
    B, S, _ = q.shape
    N = S // CHUNK
    dt = q.dtype
    f32 = jnp.float32
    q = rms_norm(q.reshape(B, S, SW_KV_HEADS, SW_GROUP, SW_HEAD_DIM), q_norm_w)
    k = rms_norm(k.reshape(B, S, SW_KV_HEADS, SW_HEAD_DIM), k_norm_w)
    v = v.reshape(B, S, SW_KV_HEADS, SW_HEAD_DIM)
    qb = q.reshape(B, N, CHUNK, SW_KV_HEADS, SW_GROUP, SW_HEAD_DIM)
    pad = (WINDOW_CHUNKS - 1) * CHUNK
    kp = jnp.pad(k, ((0, 0), (pad, 0), (0, 0), (0, 0)))
    vp = jnp.pad(v, ((0, 0), (pad, 0), (0, 0), (0, 0)))
    kb = jnp.concatenate([kp[:, j * CHUNK: j * CHUNK + S].reshape(B, N, CHUNK, SW_KV_HEADS, SW_HEAD_DIM)
                          for j in range(WINDOW_CHUNKS)], axis=2)
    vb = jnp.concatenate([vp[:, j * CHUNK: j * CHUNK + S].reshape(B, N, CHUNK, SW_KV_HEADS, SW_HEAD_DIM)
                          for j in range(WINDOW_CHUNKS)], axis=2)
    key_chunk = jnp.arange(N)[:, None] - (WINDOW_CHUNKS - 1) + jnp.arange(WINDOW_CHUNKS)[None, :]
    valid = jnp.repeat(key_chunk >= 0, CHUNK, axis=1)
    scale = SW_HEAD_DIM ** -0.5
    s = jnp.einsum('bnqkgd,bnskd->bnkgqs', qb, kb).astype(f32) * scale
    s = jnp.where(valid[None, :, None, None, None, :], s, -1e30)
    sink = jnp.broadcast_to(sinks.astype(f32).reshape(SW_KV_HEADS, SW_GROUP)[None, None, :, :, None, None],
                            s.shape[:-1] + (1,))
    p = jax.nn.softmax(jnp.concatenate([s, sink], axis=-1), axis=-1)[..., :-1]
    o = jnp.einsum('bnkgqs,bnskd->bnqkgd', p.astype(dt), vb)
    return o.reshape(B, S, SW_WIDTH)

def peer_ffn(h, w_query, sub_keys, expert_u, expert_v):
    B, S, D = h.shape
    T = B * S
    f32 = jnp.float32
    blocks = h.reshape(T // PEER_BLOCK, PEER_BLOCK, D)

    def block(xb):
        qy = (xb @ w_query).reshape(PEER_BLOCK, PEER_HEADS, 2, PEER_DQ // 2)
        s = jnp.einsum('phcd,hckd->phck', qy, sub_keys).astype(f32)
        top_s, top_i = lax.top_k(s, PEER_TOPK)
        cand_s = top_s[:, :, 0, :, None] + top_s[:, :, 1, None, :]
        cand_i = top_i[:, :, 0, :, None] * N_KEYS + top_i[:, :, 1, None, :]
        best_s, best_j = lax.top_k(cand_s.reshape(PEER_BLOCK, PEER_HEADS, PEER_TOPK * PEER_TOPK), PEER_TOPK)
        experts = jnp.take_along_axis(cand_i.reshape(PEER_BLOCK, PEER_HEADS, PEER_TOPK * PEER_TOPK),
                                      best_j, axis=-1)
        gate = jax.nn.softmax(best_s, axis=-1)
        u = expert_u[experts]
        v = expert_v[experts]
        act = jax.nn.gelu(jnp.einsum('pd,phkd->phk', xb, u), approximate=False)
        return jnp.einsum('phk,phkd->pd', (gate * act.astype(f32)).astype(xb.dtype), v)

    return lax.map(block, blocks).reshape(B, S, D)

def setup_inputs(seed: int = 0) -> dict:
    key = jax.random.key(seed)
    ks = jax.random.split(key, 20)
    nrm = jax.random.normal
    f32 = jnp.float32
    return {
        "x": nrm(ks[0], (BATCH, SEQ, D_MODEL), f32),
        "c": nrm(ks[1], (BATCH, D_MODEL), f32),
        "w_ada": nrm(ks[2], (DEPTH, D_MODEL, N_MOD * D_MODEL), f32) * (0.5 * D_MODEL ** -0.5),
        "b_ada": nrm(ks[3], (DEPTH, N_MOD * D_MODEL), f32) * 0.01,
        "norm_mix_w": 1.0 + 0.02 * nrm(ks[4], (DEPTH, D_MODEL), f32),
        "w_in": nrm(ks[5], (DEPTH, D_MODEL, D_IN), f32) * D_MODEL ** -0.5,
        "hg_lb_raw": 0.5 * nrm(ks[6], (DEPTH + 1, HG_HEADS * HG_DK), f32),
        "hg_norm_w": 1.0 + 0.02 * nrm(ks[7], (DEPTH, HG_DV), f32),
        "q_norm_w": 1.0 + 0.02 * nrm(ks[8], (DEPTH, SW_HEAD_DIM), f32),
        "k_norm_w": 1.0 + 0.02 * nrm(ks[9], (DEPTH, SW_HEAD_DIM), f32),
        "sinks": 0.5 * nrm(ks[10], (DEPTH, SW_HEADS), f32),
        "w_branch": nrm(ks[11], (DEPTH, N_BRANCH, BRANCH_WIDTH, D_MODEL), f32) * BRANCH_WIDTH ** -0.5,
        "w_out": nrm(ks[12], (DEPTH, D_MODEL, D_MODEL), f32) * D_MODEL ** -0.5,
        "norm_ffn_w": 1.0 + 0.02 * nrm(ks[13], (DEPTH, D_MODEL), f32),
        "w_query": nrm(ks[14], (DEPTH, D_MODEL, PEER_HEADS * PEER_DQ), f32) * D_MODEL ** -0.5,
        "sub_keys": nrm(ks[15], (DEPTH, PEER_HEADS, 2, N_KEYS, PEER_DQ // 2), f32) * (PEER_DQ // 2) ** -0.5,
        "expert_u": nrm(ks[16], (DEPTH, N_EXPERTS, D_MODEL), f32) * D_MODEL ** -0.5,
        "expert_v": nrm(ks[17], (DEPTH, N_EXPERTS, D_MODEL), f32) * 0.5,
    }

def reference(x, c, w_ada, b_ada, norm_mix_w, w_in, hg_lb_raw, hg_norm_w, q_norm_w, k_norm_w,
              sinks, w_branch, w_out, norm_ffn_w, w_query, sub_keys, expert_u, expert_v):
    B, S, D = x.shape
    split_points = np.cumsum(SPLIT_SIZES)[:-1].tolist()
    lb_all = jnp.cumsum(jax.nn.softmax(hg_lb_raw.astype(jnp.float32), axis=0), axis=0)
    c_act = jax.nn.silu(c)
    for l in range(DEPTH):
        mod = c_act @ w_ada[l] + b_ada[l]
        shift1, scale1, gate1, shift2, scale2, gate2 = jnp.split(mod[:, None, :], N_MOD, axis=-1)

        h = rms_norm(x, norm_mix_w[l]) * (1.0 + scale1) + shift1
        proj = h @ w_in[l]
        hq, hf, hi, hg, sq, sk, sv, gl = jnp.split(proj, split_points, axis=-1)
        y_hg = hgrn2_mix(hq, hf, hi, hg, lb_all[l], hg_norm_w[l])
        y_sw = swa_sink_mix(sq, sk, sv, q_norm_w[l], k_norm_w[l], sinks[l])
        branches = jnp.stack([y_hg, y_sw], axis=2)
        y = jnp.einsum('bsnw,nwd->bsnd', branches, w_branch[l])
        merge = jax.nn.sigmoid(gl.reshape(B, S, N_BRANCH, D))
        mixed = jnp.sum(merge * y, axis=2) @ w_out[l]
        x = x + gate1 * mixed

        h2 = rms_norm(x, norm_ffn_w[l]) * (1.0 + scale2) + shift2
        x = x + gate2 * peer_ffn(h2, w_query[l], sub_keys[l], expert_u[l], expert_v[l])
    return x


_drawn_inputs = setup_inputs


def setup_inputs(seed=0):
    import zlib

    import numpy as np

    out = dict(_drawn_inputs(seed))
    spreads = {}
    factors = {'b_ada': 4.779,
     'norm_mix_w': 7.871,
     'hg_norm_w': 8.0,
     'q_norm_w': 8.0,
     'k_norm_w': 8.0,
     'sinks': 8.0,
     'norm_ffn_w': 37.552}
    for name, (base, spread) in spreads.items():
        noise = np.random.default_rng([zlib.crc32(name.encode()), seed]).standard_normal(out[name].shape)
        drawn = base * np.exp(spread * noise) if base else spread * noise
        out[name] = __import__('jax').numpy.asarray(drawn.astype(out[name].dtype))
    for name, factor in factors.items():
        out[name] = (out[name] * factor).astype(out[name].dtype)
    return out
```

```python
import numpy as np
import concourse.bass as bass
from concourse import mybir
from contextlib import ExitStack, contextmanager

F32 = mybir.dt.float32
F32R = mybir.dt.float32r
I32 = mybir.dt.int32
U32 = mybir.dt.uint32
ALU = mybir.AluOpType
ACT = mybir.ActivationFunctionType
AX = mybir.AxisListType.X

P = 128
D = 1024
T = 1024
KD = D // P
TT = T // P
HALF = 512
D_IN = 4864
COL_HQ, COL_HF, COL_HI, COL_HG, COL_SQ, COL_SK, COL_SV, COL_GL = 0, 512, 1024, 1536, 2048, 2560, 2688, 2816
N_MOD = 6
EPS = 1e-6
NH = 4
SWH, SWKV, HD = 8, 2, 64
HEADS, TOPK, NKEYS = 8, 16, 128
NEG = -1e30


class Chain:

    def __init__(self, eng, sem):
        self.eng, self.sem, self.start, self.n, self.base = eng, sem, 0, 0, 0

    def __call__(self, ins, *signals):
        self.n += 1
        ins.then_inc(self.sem, 1)
        self.eng.wait_ge(self.sem, self.base + self.n)
        for s in signals:
            self.eng.sem_inc(s, 1)

    def enter(self, turn, per):
        self.start += self.n
        self.base, self.n, self.per = self.start + turn * per, 0, per

    def leave(self, turns):
        assert self.n == self.per, (self.n, self.per)
        self.start += self.per * turns
        self.base, self.n = self.start, 0


class Steps:

    def __init__(self, sem, slots, unit=1):
        self.sem, self.slots, self.unit = sem, slots, unit

    def open(self, eng):
        eng.sem_inc(self.sem, self.slots * self.unit)

    def done(self, n):
        return n * self.unit + (self.slots + 1) * self.unit

    def free(self, n):
        return n * self.unit + self.unit


def settle(eng, sem):
    eng.sem_inc(sem, 1)


@contextmanager
def phase_semaphores(nc):
    with ExitStack() as ctx:
        taken = []

        def sem(name):
            taken.append(ctx.enter_context(nc.semaphore(name)))
            return taken[-1]

        yield sem
        with nc.Block() as block:
            @block.gpsimd
            def _(pool):
                for one in taken:
                    pool.sem_clear(one)


def setup_phase(nc, io, keep):
    NB = N_MOD * D // HALF
    CH = HALF // P
    with ExitStack() as ctx:
        sem = ctx.enter_context(phase_semaphores(nc))
        sb = lambda n, s, d=F32: ctx.enter_context(nc.sbuf_tensor(n, s, d))
        ps = lambda n, s: ctx.enter_context(nc.psum_tensor(n, s, F32))
        prow = sb("prow", [P, P])
        wada = sb("wada", [P, 2, KD, HALF])
        csig = sb("csig", [P, KD])
        cact = sb("cact", [P, KD])
        modt = sb("modt", [6 * KD, P])
        pp = ps("pp", [P, P])
        pm = [ps(f"pm{i}", [P, CH]) for i in range(2)]
        pt = ps("pt", [6 * KD, P])
        par_in, wada_in = sem("par_in"), [sem(f"wada_in{i}") for i in range(2)]
        id_done, par_t, par_cp, sig_done = sem("id_done"), sem("par_t"), sem("par_cp"), sem("sig_done")
        cact_done, mod_mm, mod_add = sem("cact_done"), Steps(sem("mod_mm"), 2), Steps(sem("mod_add"), 2)
        a1_done, modT_t, modT_cp, mod_st = sem("a1_done"), sem("modT_t"), sem("modT_cp"), sem("mod_st")
        lbd_done = sem("lbd_done")
        K = keep
        NPAR = 8 + 8 + 8 + 48 + 8
        wv = io["w_ada"][0].rearrange("(k p) n -> p k n", p=P)
        with nc.Block() as block:
            @block.sync
            def _(sp):
                for steps in (mod_mm, mod_add):
                    steps.open(sp)
                rows = [(io["c"][0].rearrange("(a b) -> a b", b=P), 8),
                        (io["norm_mix_w"][0].rearrange("(a b) -> a b", b=P), 8),
                        (io["norm_ffn_w"][0].rearrange("(a b) -> a b", b=P), 8),
                        (io["b_ada"][0].rearrange("(a b) -> a b", b=P), 48),
                        (io["hg_lb_raw"].rearrange("l (a b) -> (l a) b", b=P), 8)]
                at = 0
                for src, n in rows:
                    sp.dma_start(prow[at:at + n, :], src).then_inc(par_in, 16)
                    at += n
                sp.dma_start(K.hgw[:, :], io["hg_norm_w"][0:1, :].to_broadcast([P, P])).then_inc(par_in, 16)
                sp.dma_start(K.qw[:, :], io["q_norm_w"][0:1, :].to_broadcast([P, HD])).then_inc(par_in, 16)
                sp.dma_start(K.kw[:, :], io["k_norm_w"][0:1, :].to_broadcast([P, HD])).then_inc(par_in, 16)
                sp.dma_start(K.sink[:, :], io["sinks"][0:1, :].to_broadcast([P, SWH])).then_inc(par_in, 16)
                with sp.Fori(0, NB // 2) as turn:
                    b = turn * 2
                    for s in range(2):
                        sp.wait_ge(mod_mm.sem, mod_mm.free(b + s))
                        sp.dma_start(wada[:, s], wv[:, :, bass.ds((b + s) * HALF, HALF)]).then_inc(wada_in[s], 16)
                sp.wait_ge(modT_cp, 1)
                sp.dma_start(io["mod_dram"].rearrange("(a b) -> a b", b=P), modt[:, :]).then_inc(mod_st, 16)
                sp.wait_ge(mod_st, 16)

            @block.gpsimd
            def _(pool):
                link = Chain(pool, sem("pool_setup"))
                link(pool.memset(K.ident[:, :], 0.0))
                link(pool.affine_select(out=K.ident[:, :], in_=K.ident[:, :], compare_op=ALU.not_equal, fill=1.0,
                                        base=0, pattern=[[-1, P]], channel_multiplier=1))
                pool.tensor_copy(K.identr[:, :], K.ident[:, :]).then_inc(id_done, 1)
                pool.iota(K.iota[:, :], pattern=[[1, P]], base=0, channel_multiplier=0,
                          allow_small_or_imprecise_dtypes=True).then_inc(id_done, 1)

            @block.tensor
            def _(pe):
                pe.wait_ge(id_done, 2)
                pe.wait_ge(par_in, 16 * 9)
                pe.transpose(pp[:, 0:NPAR], prow[0:NPAR, :], K.ident[0:NPAR, 0:NPAR]).then_inc(par_t, 1)
                pe.wait_ge(cact_done, 1)
                with pe.Fori(0, NB // 2) as turn:
                    b = turn * 2
                    for s in range(2):
                        pe.wait_ge(wada_in[s], b * 8 + 16)
                        pe.wait_ge(mod_add.sem, mod_add.free(b + s))
                        for j in range(CH):
                            for k in range(KD):
                                last = pe.matmul(pm[s][:, j:j + 1], wada[:, s, k, j * P:(j + 1) * P], cact[:, k:k + 1],
                                                 start=(k == 0), stop=(k == KD - 1))
                        last.then_inc(mod_mm.sem, 1)
                pe.wait_ge(a1_done, 1)
                pe.transpose(pt[:, :], K.mod[:, :], K.ident[:, :]).then_inc(modT_t, 1)

            @block.scalar
            def _(act):
                act.wait_ge(par_cp, 1)
                act.activation(csig[:, :], K.par[:, 0:8], ACT.Sigmoid).then_inc(sig_done, 1)
                act.wait_ge(lbd_done, 1)
                act.activation(K.lbs[:, :], K.lbd[:, :], ACT.Sigmoid).then_inc(sig_done, 1)

            @block.vector
            def _(dve):
                link = Chain(dve, sem("dve_setup"))
                dve.memset(K.eps[:, :], EPS)
                dve.wait_ge(par_t, 1)
                dve.tensor_copy(K.par[:, 0:NPAR], pp[:, 0:NPAR]).then_inc(par_cp, 1)
                dve.wait_ge(sig_done, 1)
                dve.tensor_tensor(cact[:, :], K.par[:, 0:8], csig[:, :], ALU.mult).then_inc(cact_done, 1)
                dve.tensor_tensor(K.lbd[:, :], K.par[:, 72:76], K.par[:, 76:80], ALU.subtract).then_inc(lbd_done, 1)
                with dve.Fori(0, NB // 2) as turn:
                    b = turn * 2
                    for s in range(2):
                        dve.wait_ge(mod_mm.sem, mod_mm.done(b + s))
                        dve.tensor_tensor(K.mod[:, bass.ds((b + s) * CH, CH)], pm[s][:, :],
                                          K.par[:, bass.ds((b + s) * CH + 24, CH)], ALU.add).then_inc(mod_add.sem, 1)
                dve.wait_ge(mod_add.sem, mod_add.done(NB - 1))
                for w, sc, out in ((8, 8, K.a1), (16, 32, K.a2)):
                    link(dve.tensor_scalar(out[:, :], K.mod[:, sc:sc + 8], 1.0, None, ALU.add))
                    link(dve.tensor_tensor(out[:, :], out[:, :], K.par[:, w:w + 8], ALU.mult))
                dve.sem_inc(a1_done, 1)
                dve.wait_ge(modT_t, 1)
                dve.tensor_copy(modt[:, :], pt[:, :]).then_inc(modT_cp, 1)


def norm_phase(nc, tag, src, a, shift, hhi, hlo, keep):
    K = keep
    with ExitStack() as ctx:
        sem = ctx.enter_context(phase_semaphores(nc))
        sb = lambda n, s, d=F32: ctx.enter_context(nc.sbuf_tensor(n + tag, s, d))
        x = sb("nx", [P, 4, D])
        sq = sb("nsq", [P, D])
        ssq = sb("nssq", [P, 4])
        rstd = sb("nrstd", [P, 4])
        hf = sb("nhf", [P, 2, HALF])
        pt = [ctx.enter_context(nc.psum_tensor(f"npt{tag}{i}", [P, HALF], F32)) for i in range(2)]
        x_in, ssq_done, root_done = sem("x_in" + tag), sem("ssq_done" + tag), sem("root_done" + tag)
        xs_done = Steps(sem("xs_done" + tag), 1)
        xT_done, hf_done, hi_done, lo_done = (Steps(sem(n + tag), 2) for n in ("xT_done", "hf_done", "hi_done", "lo_done"))
        with nc.Block() as block:
            @block.sync
            def _(sp):
                for steps in (xs_done, xT_done, hf_done, hi_done, lo_done):
                    steps.open(sp)
                for g in range(2):
                    if g:
                        sp.wait_ge(xT_done.sem, xT_done.done(KD - 1))
                    sp.dma_start(x[:, :, :], src[g * HALF:(g + 1) * HALF, :].rearrange("(t p) d -> p t d", p=P)).then_inc(x_in, 16)

            @block.scalar
            def _(act):
                with act.Fori(0, 2) as g:
                    act.wait_ge(x_in, g * 16 + 16)
                    act.wait_ge(xs_done.sem, xs_done.free(g))
                    for t in range(4):
                        act.activation(sq[:, :], x[:, t], ACT.Square, accum_out=ssq[:, t:t + 1]).then_inc(ssq_done, 1)
                        act.wait_ge(ssq_done, g * 4 + (t + 1))
                    act.activation(rstd[:, :], ssq[:, :], ACT.Sqrt, bias=K.eps[:, :], scale=1.0 / D).then_inc(root_done, 1)
                    for k in range(KD):
                        act.wait_ge(hf_done.sem, hf_done.done(g * KD + k))
                        act.activation(hhi[:, k, bass.ds(g * HALF, HALF)], hf[:, k % 2], ACT.Copy).then_inc(hi_done.sem, 1)

            @block.vector
            def _(dve):
                link = Chain(dve, sem("dve_norm" + tag))
                with dve.Fori(0, 2) as g:
                    link.enter(g, 5 + 2 * KD)
                    dve.wait_ge(root_done, g + 1)
                    link(dve.reciprocal(rstd[:, :], rstd[:, :]))
                    for t in range(4):
                        link(dve.tensor_scalar(x[:, t], x[:, t], rstd[:, t:t + 1], None, ALU.mult), *[xs_done.sem] * (t == 3))
                    for k in range(KD + 1):
                        if k < KD:
                            dve.wait_ge(xT_done.sem, xT_done.done(g * KD + k))
                            link(dve.tensor_scalar(hf[:, k % 2], pt[k % 2][:, :], a[:, k:k + 1], shift[:, k:k + 1],
                                                   ALU.mult, ALU.add), hf_done.sem)
                        if k:
                            dve.wait_ge(hi_done.sem, hi_done.done(g * KD + (k - 1)))
                            link(dve.tensor_tensor(hlo[:, k - 1, bass.ds(g * HALF, HALF)], hf[:, (k - 1) % 2],
                                                   hhi[:, k - 1, bass.ds(g * HALF, HALF)].bitcast(F32), ALU.subtract), lo_done.sem)
                link.leave(2)

            @block.tensor
            def _(pe):
                with pe.Fori(0, 2) as g:
                    pe.wait_ge(xs_done.sem, xs_done.done(g))
                    for k in range(KD):
                        pe.wait_ge(hf_done.sem, hf_done.free(g * KD + k))
                        for t in range(4):
                            last = pe.transpose(pt[k % 2][:, t * P:(t + 1) * P], x[:, t, k * P:(k + 1) * P], K.ident[:, :])
                        last.then_inc(xT_done.sem, 1)


def three_pass(pe, out, lhi, llo, rhi, rlo, k, n):
    pe.matmul(out, lhi, rhi, start=(k == 0), stop=False)
    pe.matmul(out, lhi, rlo, start=False, stop=False)
    return pe.matmul(out, llo, rhi, start=False, stop=(k == n - 1))


def token_gemm_phase(nc, tag, hhi, hlo, nk, wsrc, width, blocks, dst):
    with ExitStack() as ctx:
        sem = ctx.enter_context(phase_semaphores(nc))
        sb = lambda n, s, d=F32: ctx.enter_context(nc.sbuf_tensor(n + tag, s, d))
        w = sb("gw", [P, 2, nk, width])
        whi = sb("gwhi", [P, 2, nk, width], F32R)
        wlo = sb("gwlo", [P, 2, nk, width], F32R)
        y = sb("gy", [P, 4, width])
        py = [ctx.enter_context(nc.psum_tensor(f"gpy{tag}{i}", [P, HALF], F32)) for i in range(4)]
        w_in = [sem(f"w_in{tag}{i}") for i in range(2)]
        hi_done, lo_done = Steps(sem("whi_done" + tag), 2), Steps(sem("wlo_done" + tag), 2)
        y_mm, y_cp = Steps(sem("y_mm" + tag), 2 * TT), Steps(sem("y_cp" + tag), 4)
        y_out = [Steps(sem(f"y_out{tag}{i}"), 1, 16) for i in range(4)]
        with nc.Block() as block:
            @block.gpsimd
            def _(pool):
                for steps in (hi_done, lo_done, y_mm, y_cp, *y_out):
                    steps.open(pool)
                with pool.Fori(0, blocks // 2) as turn:
                    b = turn * 2
                    for s in range(2):
                        pool.wait_ge(lo_done.sem, lo_done.free(b + s))
                        pool.dma_start(w[:, s], wsrc[:, :, bass.ds((b + s) * width, width)]).then_inc(w_in[s], 16)

            @block.scalar
            def _(act):
                def cut_high(b, s):
                    act.wait_ge(w_in[s], b * 8 + 16)
                    act.wait_ge(y_mm.sem, y_mm.free((b + s) * TT + TT - 1))
                    act.activation(whi[:, s], w[:, s], ACT.Copy).then_inc(hi_done.sem, 1)

                with act.Fori(0, blocks // 2) as turn:
                    b = turn * 2
                    for s in range(2):
                        cut_high(b, s)

            @block.vector
            def _(dve):
                def cut_low(b, s):
                    dve.wait_ge(hi_done.sem, hi_done.done(b + s))
                    dve.tensor_tensor(wlo[:, s], w[:, s], whi[:, s].bitcast(F32), ALU.subtract).then_inc(lo_done.sem, 1)

                def copy_out(b, s):
                    for t in range(TT):
                        dve.wait_ge(y_mm.sem, y_mm.done((b + s) * TT + t))
                        dve.wait_ge(y_out[t % 4].sem, y_out[t % 4].free((b + s) * 2 + t // 4))
                        dve.tensor_copy(y[:, t % 4], py[t % 4][:, 0:width]).then_inc(y_cp.sem, 1)

                for s in range(2):
                    cut_low(0, s)
                if blocks > 2:
                    with dve.Fori(0, blocks // 2 - 1) as turn:
                        b = turn * 2
                        for s in range(2):
                            copy_out(b, s)
                            cut_low(b + 2, s)
                for s in range(2):
                    copy_out(blocks - 2, s)

            @block.sync
            def _(sp):
                with sp.Fori(0, blocks // 2) as turn:
                    b = turn * 2
                    for s in range(2):
                        for t in range(TT):
                            sp.wait_ge(y_cp.sem, y_cp.done((b + s) * TT + t))
                            sp.dma_start(dst[t * P:(t + 1) * P, bass.ds((b + s) * width, width)], y[:, t % 4]).then_inc(y_out[t % 4].sem, 16)
                for i in range(4):
                    sp.wait_ge(y_out[i].sem, y_out[i].done(2 * blocks - 1))

            @block.tensor
            def _(pe):
                with pe.Fori(0, blocks // 2) as turn:
                    b = turn * 2
                    for s in range(2):
                        pe.wait_ge(lo_done.sem, lo_done.done(b + s))
                        for t in range(TT):
                            pe.wait_ge(y_cp.sem, y_cp.free((b + s) * TT + t))
                            for k in range(nk):
                                last = three_pass(pe, py[t % 4][:, 0:width], hhi[:, k, t * P:(t + 1) * P], hlo[:, k, t * P:(t + 1) * P],
                                                  whi[:, s, k], wlo[:, s, k], k, nk)
                            last.then_inc(y_mm.sem, 1)


def place(head):
    return (head % 2) * 4 + head // 2


LEVELS = [64, 32, 16, 8, 4, 2, 1]


def mixer_phase(nc, proj, yhi, ylo, keep):
    K = keep
    W = COL_GL
    with ExitStack() as ctx:
        sem = ctx.enter_context(phase_semaphores(nc))
        sb = lambda n, s, d=F32: ctx.enter_context(nc.sbuf_tensor(n, s, d))
        prj = sb("prj", [P, 2, W])
        masks = sb("masks", [P, len(LEVELS) + 1, P], I32)
        mt = sb("mt", [P, 3, P], I32)
        ti, si = sb("ti", [P, P], I32), sb("si", [P, P], I32)
        reset = sb("reset", [P, NH * P])
        lb, omlb = sb("lb", [P, NH]), sb("omlb", [P, NH])
        qT, kT, fT, lf, b = (sb(n, [P, NH, P]) for n in ("hqT", "hkT", "hfT", "hlf", "hb"))
        dif, ex, wl = sb("dif", [P, 2, NH * P]), sb("ex", [P, 2, NH * P]), sb("wl", [P, 2, NH, P])
        S = sb("hS", [P, NH, P])
        E0, qd, kd, kdt, dl = (sb(n, [P, NH, P]) for n in ("hE0", "hqd", "hkd", "hkdt", "hdl"))
        state = sb("state", [P, NH, P])
        o, osq, sg = sb("ho", [P, NH, P]), sb("hosq", [P, NH * P]), sb("hsg", [P, NH * P])
        oss = sb("hoss", [P, NH])
        y2 = sb("y2", [P, 2, 512])
        sqb, ss10 = sb("sqb", [P, 640]), sb("ss10", [P, 10])
        qkn = sb("qkn", [P, 10, HD])
        kk = sb("kk", [P, SWKV, 2, HD])
        qT2 = sb("qT2", [P, 4, P])
        kTs = sb("kTs", [P, 2, SWKV, P])
        vr = sb("vr", [P, 2, P])
        pm = sb("pm", [HD, HD])
        sc = sb("sc", [P, SWH, 193])
        pb = sb("pb", [P, SWH, 257])
        mx, den = sb("smx", [P, SWH]), sb("sden", [P, SWH])
        pTc, pTp = sb("pTc", [P, SWH, P]), sb("pTp", [P, SWH, P])
        yf = sb("yf", [P, 8, P])
        bk = [ctx.enter_context(nc.psum_tensor(f"mbk{i}", [P, HALF], F32)) for i in range(4)]
        big = ctx.enter_context(nc.psum_tensor("mbig", [P, SWH, 256], F32))

        prj_in = [sem(f"prj_in{i}") for i in range(2)]
        names = ("tile_done", "hgT_mm", "q_cp", "sig_done", "f_done", "log_done", "e0_done", "kd_ready", "kdT_mm", "kdT_cp",
                 "s_done", "qd_done", "o_mm", "su_mm", "osq_done", "ssig_done", "oroot", "oss_done", "sq_done", "ss_done", "qkroot",
                 "qk_ready", "swT_mm", "qT2_cp", "kT2_cp", "sc_mm", "sc_low", "sc_all", "negmax", "exp_done", "pT_mm", "pTc_cp",
                 "pTp_cp", "osw_mm", "y_done", "yT_mm", "yhi_done", "blast_dif", "blast_ex", "gsg_done", "prep", "den_done")
        s = {n: sem("m_" + n) for n in names}
        tile_free = Steps(sem("tile_free"), 2)
        dif_done, ex_done, wl_done = sem("dif_done"), sem("ex_done"), sem("wl_done")
        lev_mm = Steps(sem("lev_mm"), 2)
        lev_used = Steps(sem("lev_used"), 2)
        state_up, yf_done = Steps(sem("state_up"), 1), Steps(sem("yf_done"), 1)
        NL = len(LEVELS)
        settled = sem("m_settled")
        with nc.Block() as block:
            @block.sync
            def _(sp):
                for steps in (tile_free, lev_mm, lev_used, state_up, yf_done):
                    steps.open(sp)
                with sp.Fori(0, TT // 2) as turn:
                    for p in range(2):
                        sp.wait_ge(tile_free.sem, tile_free.free(turn * 2 + p))
                        sp.dma_start(prj[:, p], proj[bass.ds((turn * 2 + p) * P, P), 0:W]).then_inc(prj_in[p], 16)

            @block.gpsimd
            def _(pool):
                link = Chain(pool, sem("pool_mix"))
                link(pool.iota(ti[:, :], pattern=[[1, P]], base=0, channel_multiplier=0))
                link(pool.iota(si[:, :], pattern=[[0, P]], base=0, channel_multiplier=1))
                link(pool.memset(state[:, :, :], 0.0))
                link(pool.memset(kTs[:, :, :, :], 0.0))
                link(pool.memset(vr[:, :, :], 0.0))
                link(pool.memset(pm[:, :], NEG))
                link(pool.memset(pb[:, :, :], 0.0))
                link(pool.memset(sc[:, :, :], NEG))
                link(pool.memset(reset[:, :], 1.0))
                link(pool.memset(reset[:, :].rearrange("p (h t) -> p h t", h=NH)[:, :, 0:1], 0.0))
                link(pool.memset(S[:, :, :], 0.0))
                link(pool.tensor_copy(sc[:, :, 192:193].rearrange("p (c j) one -> p j c one", c=2),
                                      K.sink[:, :, None].rearrange("p (j c) one -> p j c one", c=2)), s["prep"])

            @block.scalar
            def _(act):
                link = Chain(act, sem("act_mix"))
                act.wait_ge(s["prep"], 2)
                with act.Fori(0, TT // 2) as turn:
                    link.enter(turn, 2 * PER_ACT)
                    for p in range(2):
                        t = turn * 2 + p
                        n = t + 1
                        act.wait_ge(s["hgT_mm"], n)
                        link(act.activation(fT[:, :, :], bk[1][:, :].rearrange("p (h t) -> p h t", h=NH), ACT.Sigmoid), s["sig_done"])
                        act.wait_ge(s["f_done"], n)
                        link(act.activation(lf[:, :, :], fT[:, :, :], ACT.Ln), s["log_done"])
                        for l, m in enumerate(LEVELS):
                            act.wait_ge(dif_done, t * NL + (l + 1))
                            dv = dif[:, l % 2].rearrange("p (n w) -> p n w", w=2 * m)
                            ev = ex[:, l % 2].rearrange("p (n w) -> p n w", w=2 * m)
                            link(act.activation(ev[:, :, 0:m], dv[:, :, 0:m], ACT.Exp, scale=-1.0))
                            link(act.activation(ev[:, :, m:], dv[:, :, m:], ACT.Exp), ex_done)
                        link(act.activation(E0[:, :, :], b[:, :, :], ACT.Exp), s["e0_done"])
                        act.wait_ge(s["blast_dif"], n)
                        link(act.activation(kd[:, :, :], dl[:, :, :], ACT.Exp, scale=-1.0), s["blast_ex"])
                        act.wait_ge(s["kdT_mm"], n)
                        link(act.activation(kdt[:, :, :], bk[1][:, :].rearrange("p (h t) -> p h t", h=NH), ACT.Copy), s["kdT_cp"])
                        link(act.activation(sqb[:, :], prj[:, p, COL_SQ:COL_SQ + 640], ACT.Square), s["sq_done"])
                        link(act.activation(vr[:, p], prj[:, p, COL_SV:COL_SV + P], ACT.Copy))
                        link(act.activation(sg[:, :], prj[:, p, COL_HG:COL_HG + 512], ACT.Sigmoid), s["gsg_done"])
                        act.wait_ge(s["ss_done"], n)
                        link(act.activation(ss10[:, :], ss10[:, :], ACT.Sqrt, bias=K.eps[:, :], scale=1.0 / HD), s["qkroot"])
                        act.wait_ge(s["o_mm"], n)
                        link(act.activation(o[:, :, :], bk[0][:, :].rearrange("p (h t) -> p h t", h=NH), ACT.Copy))
                        link(act.activation(osq[:, :], o[:, :, :].rearrange("p h t -> p (h t)"), ACT.Square), s["osq_done"])
                        act.wait_ge(s["oss_done"], n)
                        link(act.activation(oss[:, :], oss[:, :], ACT.Sqrt, bias=K.eps[:, :], scale=1.0 / P), s["oroot"])
                        act.wait_ge(s["swT_mm"], n)
                        link(act.activation(kTs[:, p], bk[3][:, 0:256].rearrange("p (g t) -> p g t", g=SWKV), ACT.Copy), s["kT2_cp"])
                        act.wait_ge(s["sc_mm"], n)
                        link(act.activation(sc[HD:P, :, HD:192], big[HD:P, :, HD:192], ACT.Copy, scale=HD ** -0.5), s["sc_low"])
                        act.wait_ge(s["negmax"], n)
                        for h in range(SWH):
                            link(act.activation(pb[:, h, 64:257], sc[:, h, :], ACT.Exp, bias=mx[:, h:h + 1], accum_out=den[:, h:h + 1]))
                        act.sem_inc(s["exp_done"], 1)
                        act.wait_ge(s["pT_mm"], n)
                        link(act.activation(pTc[:, :, :], big[:, 0:4].rearrange("p a (b t) -> p (a b) t", b=2), ACT.Copy), s["pTc_cp"])
                        act.wait_ge(yf_done.sem, yf_done.done(t))
                        link(act.activation(yhi[:, :, bass.ds(t * P, P)], yf[:, :, :], ACT.Copy), s["yhi_done"])
                link.leave(TT // 2)

            @block.vector
            def _(dve):
                link = Chain(dve, sem("dve_mix"))
                dve.wait_ge(s["prep"], 1)
                link(dve.memset(mt[:, 0], 0))
                for l, m in enumerate(LEVELS):
                    sh = m.bit_length() - 1
                    link(dve.tensor_single_scalar(mt[:, 0], ti[:, :], sh, ALU.logical_shift_right))
                    link(dve.tensor_single_scalar(mt[:, 1], si[:, :], sh, ALU.logical_shift_right))
                    link(dve.tensor_single_scalar(mt[:, 2], mt[:, 0], 1, ALU.bitwise_and))
                    link(dve.tensor_tensor(mt[:, 0], mt[:, 0], mt[:, 1], ALU.subtract))
                    link(dve.tensor_single_scalar(mt[:, 0], mt[:, 0], 1.0, ALU.is_equal))
                    link(dve.tensor_tensor(masks[:, l], mt[:, 0], mt[:, 2], ALU.mult))
                link(dve.tensor_tensor(masks[:, NL], ti[:, :], si[:, :], ALU.is_equal))
                link(dve.tensor_copy(lb[:, :], K.lbs[:, :]))
                link(dve.tensor_scalar(omlb[:, :], lb[:, :], -1.0, 1.0, ALU.mult, ALU.add), s["prep"])
                with dve.Fori(0, TT // 2) as turn:
                    link.enter(turn, 2 * PER_DVE)
                    for p in range(2):
                        t = turn * 2 + p
                        n = t + 1
                        dve.wait_ge(s["hgT_mm"], n)
                        link(dve.tensor_copy(qT[:, :, :], bk[0][:, :].rearrange("p (h t) -> p h t", h=NH)), s["q_cp"])
                        dve.wait_ge(s["sig_done"], n)
                        for h in range(NH):
                            link(dve.tensor_scalar(fT[:, h], fT[:, h], omlb[:, h:h + 1], lb[:, h:h + 1], ALU.mult, ALU.add),
                                 *[s["f_done"]] * (h == NH - 1))
                        link(dve.tensor_scalar(kT[:, :, :], fT[:, :, :], -1.0, 1.0, ALU.mult, ALU.add))
                        dve.wait_ge(s["log_done"], n)
                        bf = b[:, :, :].rearrange("p h t -> p (h t)")
                        qf, kf = (x[:, :, :].rearrange("p h t -> p (h t)") for x in (qT, kT))
                        link(dve.tensor_tensor_scan(bf, reset[:, :], lf[:, :, :].rearrange("p h t -> p (h t)"), 0.0, ALU.mult, ALU.add))

                        def level_dif(l):
                            m = LEVELS[l]
                            bv = bf.rearrange("p (n w) -> p n w", w=2 * m)
                            link(dve.tensor_tensor(dif[:, l % 2].rearrange("p (n w) -> p n w", w=2 * m), bv,
                                                   bv[:, :, m - 1:m].to_broadcast([P, NH * P // (2 * m), 2 * m]), ALU.subtract), dif_done)

                        def level_take(l):
                            dve.wait_ge(lev_mm.sem, lev_mm.done(t * (NL + 1) + l))
                            settle(dve, settled)
                            link(dve.copy_predicated(S[:, :, :], masks[:, l:l + 1, :].to_broadcast([P, NH, P]),
                                                     bk[2 + l % 2][:, :].rearrange("p (h t) -> p h t", h=NH)), lev_used.sem)

                        level_dif(0)
                        for l, m in enumerate(LEVELS):
                            if l + 1 < NL:
                                level_dif(l + 1)
                            dve.wait_ge(ex_done, t * NL + (l + 1))
                            dve.wait_ge(lev_mm.sem, lev_mm.free(t * (NL + 1) + l))
                            w = wl[:, l % 2].rearrange("p h t -> p (h t)").rearrange("p (n w) -> p n w", w=2 * m)
                            ev = ex[:, l % 2].rearrange("p (n w) -> p n w", w=2 * m)
                            kv, qv = (x.rearrange("p (n w) -> p n w", w=2 * m) for x in (kf, qf))
                            link(dve.tensor_tensor(w[:, :, 0:m], kv[:, :, 0:m], ev[:, :, 0:m], ALU.mult))
                            link(dve.tensor_tensor(w[:, :, m:], qv[:, :, m:], ev[:, :, m:], ALU.mult), wl_done)
                            if l:
                                level_take(l - 1)
                        link(dve.tensor_tensor(dl[:, :, :], b[:, :, :], b[:, :, P - 1:P].to_broadcast([P, NH, P]), ALU.subtract), s["blast_dif"])
                        dve.wait_ge(s["e0_done"], n)
                        link(dve.tensor_tensor(qd[:, :, :], qT[:, :, :], E0[:, :, :], ALU.mult), s["qd_done"])
                        dve.wait_ge(s["blast_ex"], n)
                        link(dve.tensor_tensor(kd[:, :, :], kd[:, :, :], kT[:, :, :], ALU.mult), s["kd_ready"])
                        level_take(NL - 1)
                        level_take(NL)
                        dve.sem_inc(s["s_done"], 1)
                        dve.wait_ge(s["sq_done"], n)
                        link(dve.tensor_reduce(ss10[:, :], sqb[:, :].rearrange("p (a d) -> p a d", d=HD), AX, ALU.add), s["ss_done"])
                        dve.wait_ge(s["su_mm"], n)
                        for h in range(NH):
                            link(dve.scalar_tensor_tensor(state[:, h], state[:, h], E0[:, h, P - 1:P], bk[1][:, h * P:(h + 1) * P],
                                                          ALU.mult, ALU.add), *[state_up.sem] * (h == NH - 1))
                        dve.wait_ge(s["qkroot"], n)
                        link(dve.reciprocal(ss10[:, :], ss10[:, :]))
                        link(dve.tensor_tensor(qkn[:, :, :], prj[:, p, COL_SQ:COL_SQ + 640].rearrange("p (a d) -> p a d", d=HD),
                                               ss10[:, :, None].to_broadcast([P, 10, HD]), ALU.mult))
                        link(dve.tensor_tensor(qkn[:, 0:8], qkn[:, 0:8], K.qw[:, None, :].to_broadcast([P, 8, HD]), ALU.mult))
                        for c in range(2):
                            link(dve.tensor_tensor(kk[:, :, c], qkn[:, 8:10], K.kw[:, None, :].to_broadcast([P, 2, HD]), ALU.mult),
                                 *[s["qk_ready"]] * c)
                        dve.wait_ge(s["osq_done"], n)
                        link(dve.tensor_reduce(oss[:, :], osq[:, :].rearrange("p (a d) -> p a d", d=P), AX, ALU.add), s["oss_done"])
                        dve.wait_ge(s["swT_mm"], n)
                        link(dve.tensor_copy(qT2[:, :, :], bk[2][:, :].rearrange("p (a t) -> p a t", a=4)), s["qT2_cp"])
                        dve.wait_ge(s["oroot"], n)
                        link(dve.reciprocal(oss[:, :], oss[:, :]))
                        yv = y2[:, 0].rearrange("p (h d) -> p h d", h=NH)
                        link(dve.tensor_tensor(yv, o[:, :, :], oss[:, :, None].to_broadcast([P, NH, P]), ALU.mult))
                        link(dve.tensor_tensor(yv, yv, K.hgw[:, None, :].to_broadcast([P, NH, P]), ALU.mult))
                        link(dve.tensor_tensor(y2[:, 0], y2[:, 0], prj[:, p, COL_HG:COL_HG + 512], ALU.mult))
                        dve.wait_ge(s["gsg_done"], n)
                        link(dve.tensor_tensor(y2[:, 0], y2[:, 0], sg[:, :], ALU.mult))
                        dve.wait_ge(s["sc_mm"], n)
                        link(dve.scalar_tensor_tensor(sc[0:HD, :, 0:HD], big[0:HD, :, 0:HD], HD ** -0.5,
                                                      pm[:, None, :].to_broadcast([HD, SWH, HD]), ALU.mult, ALU.add))
                        link(dve.tensor_scalar(sc[0:HD, :, HD:P], big[0:HD, :, HD:P], HD ** -0.5, None, ALU.mult))
                        link(dve.memset(pm[:, :], 0.0))
                        dve.wait_ge(s["sc_low"], n)
                        link(dve.tensor_reduce(mx[:, :], sc[:, :, :], AX, ALU.max))
                        link(dve.tensor_scalar(mx[:, :], mx[:, :], -1.0, None, ALU.mult), s["negmax"])
                        dve.wait_ge(s["pT_mm"], n)
                        link(dve.tensor_copy(pTp[:, :, :], big[:, 4:8].rearrange("p a (b t) -> p (a b) t", b=2)), s["pTp_cp"])
                        dve.wait_ge(s["exp_done"], n)
                        link(dve.reciprocal(den[:, :], den[:, :]))
                        dve.wait_ge(s["osw_mm"], n)
                        link(dve.tensor_tensor(y2[:, 1].rearrange("p (j c d) -> p j c d", c=2, d=HD),
                                               bk[2][:, :].rearrange("p (j c d) -> p j c d", c=2, d=HD),
                                               den[:, :, None].rearrange("p (c j) one -> p j c one", c=2).to_broadcast([P, 4, 2, HD]),
                                               ALU.mult), s["y_done"], tile_free.sem)
                        dve.wait_ge(s["yT_mm"], n)
                        for c in range(2):
                            link(dve.tensor_copy(yf[:, 4 * c:4 * c + 4], bk[3 * c][:, :].rearrange("p (a t) -> p a t", a=4)),
                                 *[yf_done.sem] * c)
                        dve.wait_ge(s["yhi_done"], n)
                        link(dve.tensor_tensor(ylo[:, :, bass.ds(t * P, P)], yf[:, :, :], yhi[:, :, bass.ds(t * P, P)].bitcast(F32), ALU.subtract))
                link.leave(TT // 2)

            @block.tensor
            def _(pe):
                with pe.Fori(0, TT // 2) as turn:
                    for p in range(2):
                        t = turn * 2 + p
                        n = t + 1
                        pe.wait_ge(prj_in[p], turn * 16 + 16)
                        pe.wait_ge(state_up.sem, state_up.free(t))
                        pe.wait_ge(yf_done.sem, yf_done.free(t))
                        for c in range(2):
                            for h in range(NH):
                                last = pe.transpose(bk[c][:, h * P:(h + 1) * P], prj[:, p, c * 512 + h * P:c * 512 + (h + 1) * P], K.ident[:, :])
                        last.then_inc(s["hgT_mm"], 1)
                        for l in range(NL + 1):
                            if l < NL:
                                pe.wait_ge(wl_done, t * NL + (l + 1))
                            pe.wait_ge(lev_used.sem, lev_used.free(t * (NL + 1) + l))
                            for h in range(NH):
                                lhs, rhs = (wl[:, l % 2, h], wl[:, l % 2, h]) if l < NL else (kT[:, h], qT[:, h])
                                last = pe.matmul(bk[2 + l % 2][:, h * P:(h + 1) * P], lhs, rhs, start=True, stop=True)
                            last.then_inc(lev_mm.sem, 1)
                        pe.wait_ge(s["kd_ready"], n)
                        for h in range(NH):
                            last = pe.transpose(bk[1][:, h * P:(h + 1) * P], kd[:, h], K.ident[:, :])
                        last.then_inc(s["kdT_mm"], 1)
                        pe.wait_ge(s["s_done"], n)
                        pe.wait_ge(s["qd_done"], n)
                        for h in range(NH):
                            v = prj[:, p, COL_HI + h * P:COL_HI + (h + 1) * P]
                            pe.matmul(bk[0][:, h * P:(h + 1) * P], S[:, h], v, start=True, stop=False)
                            last = pe.matmul(bk[0][:, h * P:(h + 1) * P], qd[:, h], state[:, h], start=False, stop=True)
                        last.then_inc(s["o_mm"], 1)
                        pe.wait_ge(s["kdT_cp"], n)
                        for h in range(NH):
                            last = pe.matmul(bk[1][:, h * P:(h + 1) * P], kdt[:, h], prj[:, p, COL_HI + h * P:COL_HI + (h + 1) * P],
                                             start=True, stop=True)
                        last.then_inc(s["su_mm"], 1)
                        pe.wait_ge(s["qk_ready"], n)
                        for a in range(4):
                            pe.transpose(bk[2][:, a * P:(a + 1) * P], qkn[:, 2 * a:2 * a + 2].rearrange("p a d -> p (a d)"), K.ident[:, :])
                        for g in range(SWKV):
                            last = pe.transpose(bk[3][:, g * P:(g + 1) * P], kk[:, g].rearrange("p a d -> p (a d)"), K.ident[:, :])
                        last.then_inc(s["swT_mm"], 1)
                        pe.wait_ge(s["qT2_cp"], n)
                        pe.wait_ge(s["kT2_cp"], n)
                        for h in range(SWH):
                            r = (h % 2) * HD
                            q = qT2[r:r + HD, h // 2]
                            pe.matmul(big[:, place(h), 0:HD], q, kTs[r:r + HD, 1 - p, h // 4, HD:P], start=True, stop=True)
                            last = pe.matmul(big[:, place(h), HD:192], q, kTs[r:r + HD, p, h // 4], start=True, stop=True)
                        last.then_inc(s["sc_mm"], 1)
                        pe.wait_ge(s["exp_done"], n)
                        for h in range(SWH):
                            pe.transpose(big[:, h // 2, (h % 2) * P:(h % 2 + 1) * P], pb[:, h, P:256], K.ident[:, :])
                            last = pe.transpose(big[:, 4 + h // 2, (h % 2) * P:(h % 2 + 1) * P], pb[:, h, 0:P], K.ident[:, :])
                        last.then_inc(s["pT_mm"], 1)
                        pe.wait_ge(s["pTc_cp"], n)
                        pe.wait_ge(s["pTp_cp"], n)
                        for h in range(SWH):
                            g = (h // 4) * HD
                            pe.matmul(bk[2][:, h * HD:(h + 1) * HD], pTc[:, place(h)], vr[:, p, g:g + HD], start=True, stop=False)
                            last = pe.matmul(bk[2][:, h * HD:(h + 1) * HD], pTp[:, place(h)], vr[:, 1 - p, g:g + HD], start=False, stop=True)
                        last.then_inc(s["osw_mm"], 1)
                        pe.wait_ge(s["y_done"], n)
                        for c in range(2):
                            for a in range(4):
                                last = pe.transpose(bk[3 * c][:, a * P:(a + 1) * P], y2[:, c, a * P:(a + 1) * P], K.ident[:, :])
                        last.then_inc(s["yT_mm"], 1)


PER_ACT = 38
PER_DVE = 67


def merge_phase(nc, yhi, ylo, proj, w_branch, w_out, x, gate1_dram, x1, keep):
    K = keep
    NS = 2 * D // HALF
    with ExitStack() as ctx:
        sem = ctx.enter_context(phase_semaphores(nc))
        sb = lambda n, s, d=F32: ctx.enter_context(nc.sbuf_tensor(n, s, d))
        wr = sb("mwr", [P, 2, 4, HALF])
        whi, wlo = sb("mwhi", [P, 2, 4, HALF], F32R), sb("mwlo", [P, 2, 4, HALF], F32R)
        gl = sb("mgl", [P, 2, HALF])
        gs = sb("mgs", [P, 2, HALF])
        pr = sb("mpr", [P, 2, HALF])
        z = sb("mz", [P, TT, D])
        acc = [ctx.enter_context(nc.psum_tensor(f"mp{i}", [P, HALF], F32)) for i in range(4)]
        w_in = [sem(f"mw_in{i}") for i in range(2)]
        hi_done, lo_done = sem("mhi_done"), sem("mlo_done")
        gl_in = [sem(f"mgl_in{i}") for i in range(2)]
        z_mm, z_prod, gsig = sem("z_mm"), sem("z_prod"), sem("gsig")
        PASS = [(h, n) for h in range(2) for n in range(2)]
        with nc.Block() as block:
            @block.sync
            def _(sp):
                for i, (h, n) in enumerate(PASS):
                    if i >= 2:
                        sp.wait_ge(lo_done, i - 1)
                    sp.dma_start(wr[:, i % 2], w_branch[0, n].rearrange("(k p) d -> p k d", p=P)[:, :, h * HALF:(h + 1) * HALF]).then_inc(w_in[i % 2], 16)

            @block.gpsimd
            def _(pool):
                for i, (h, n) in enumerate(PASS):
                    for t in range(TT):
                        u = i * TT + t
                        if u >= 2:
                            pool.wait_ge(gsig, u - 1)
                        c = COL_GL + n * D + h * HALF
                        pool.dma_start(gl[:, u % 2], proj[t * P:(t + 1) * P, c:c + HALF]).then_inc(gl_in[u % 2], 16)

            @block.scalar
            def _(act):
                def cut_high(i):
                    act.wait_ge(w_in[i % 2], 16 * (i // 2 + 1))
                    if i >= 2:
                        act.wait_ge(z_mm, (i - 1) * TT)
                    act.activation(whi[:, i % 2], wr[:, i % 2], ACT.Copy).then_inc(hi_done, 1)

                cut_high(0)
                cut_high(1)
                for i in range(4):
                    for t in range(TT):
                        u = i * TT + t
                        act.wait_ge(gl_in[u % 2], 16 * (u // 2 + 1))
                        if u >= 2:
                            act.wait_ge(z_prod, u - 1)
                            act.wait_ge(gsig, u - 1)
                        act.activation(gs[:, u % 2], gl[:, u % 2], ACT.Sigmoid).then_inc(gsig, 1)
                    if i + 2 < 4:
                        cut_high(i + 2)

            @block.vector
            def _(dve):
                link = Chain(dve, sem("dve_merge"))

                def cut_low(i):
                    dve.wait_ge(hi_done, i + 1)
                    link(dve.tensor_tensor(wlo[:, i % 2], wr[:, i % 2], whi[:, i % 2].bitcast(F32), ALU.subtract), lo_done)

                cut_low(0)
                cut_low(1)
                for i, (h, n) in enumerate(PASS):
                    for t in range(TT):
                        u = i * TT + t
                        zt = z[:, t, h * HALF:(h + 1) * HALF]
                        dve.wait_ge(z_mm, u + 1)
                        dve.wait_ge(gsig, u + 1)
                        link(dve.tensor_tensor(pr[:, u % 2] if n else zt, acc[u % 4][:, :], gs[:, u % 2], ALU.mult), z_prod)
                        if n:
                            link(dve.tensor_tensor(zt, zt, pr[:, u % 2], ALU.add))
                    if i + 2 < 4:
                        cut_low(i + 2)

            @block.tensor
            def _(pe):
                for i, (h, n) in enumerate(PASS):
                    pe.wait_ge(lo_done, i + 1)
                    for t in range(TT):
                        u = i * TT + t
                        if u >= 4:
                            pe.wait_ge(z_prod, u - 3)
                        for k in range(4):
                            last = three_pass(pe, acc[u % 4][:, :], yhi[:, 4 * n + k, t * P:(t + 1) * P], ylo[:, 4 * n + k, t * P:(t + 1) * P],
                                              whi[:, i % 2, k], wlo[:, i % 2, k], k, 4)
                        last.then_inc(z_mm, 1)

        wo = wr
        pt = acc[0:2]
        zt_mm, zf_done, zhi_done = Steps(sem("zt_mm"), 2), Steps(sem("zf_done"), 2), Steps(sem("zhi_done"), 2)
        zlo_done = sem("zlo_done")
        wo_in, wohi, wolo = sem("wo_in"), sem("wohi"), sem("wolo")
        xt = sb("mxt", [P, 2, HALF])
        gate1, gate1_in = sb("gate1", [P, D]), sem("gate1_in")
        xt_in = [sem(f"xt_in{i}") for i in range(2)]
        m_read = sem("m_read")
        m_mm, m_done, x1_out = sem("m_mm"), sem("m_done"), [sem(f"x1_out{i}") for i in range(2)]
        with nc.Block() as block:
            units = [(j, t) for j in range(2) for t in range(TT)]

            @block.sync
            def _(sp):
                sp.dma_start(gate1[:, :], gate1_dram.to_broadcast([P, D])).then_inc(gate1_in, 16)
                for j in range(2):
                    if j:
                        sp.wait_ge(wolo, 2)
                    for q in range(2):
                        sp.dma_start(wo[:, q], w_out[0].rearrange("(k p) d -> p k d", p=P)[:, 4 * q:4 * q + 4, j * HALF:(j + 1) * HALF]).then_inc(wo_in, 16)
                for u, (j, t) in enumerate(units):
                    sp.wait_ge(m_done, u + 1)
                    sp.dma_start(x1[t * P:(t + 1) * P, j * HALF:(j + 1) * HALF], xt[:, u % 2]).then_inc(x1_out[u % 2], 16)
                for i in range(2):
                    sp.wait_ge(x1_out[i], 16 * TT)

            @block.gpsimd
            def _(pool):
                for u, (j, t) in enumerate(units):
                    if u >= 2:
                        pool.wait_ge(x1_out[u % 2], 16 * (u // 2))
                    pool.dma_start(xt[:, u % 2], x[t * P:(t + 1) * P, j * HALF:(j + 1) * HALF]).then_inc(xt_in[u % 2], 16)

            @block.scalar
            def _(act):
                def cut_high(j):
                    act.wait_ge(wo_in, 32 * (j + 1))
                    if j:
                        act.wait_ge(m_mm, TT)
                        act.wait_ge(wohi, 2)
                    for q in range(2):
                        act.activation(whi[:, q], wo[:, q], ACT.Copy).then_inc(wohi, 1)

                for u in range(2 * KD):
                    act.wait_ge(zf_done.sem, u + 3)
                    act.activation(yhi[:, u % KD, (u // KD) * HALF:(u // KD + 1) * HALF], gs[:, u % 2], ACT.Copy).then_inc(zhi_done.sem, 1)
                cut_high(0)
                cut_high(1)

            @block.vector
            def _(dve):
                link = Chain(dve, sem("dve_out"))
                for steps in (zt_mm, zf_done, zhi_done):
                    steps.open(dve)
                for u in range(2 * KD):
                    dve.wait_ge(zt_mm.sem, zt_mm.done(u))
                    link(dve.tensor_copy(gs[:, u % 2], pt[u % 2][:, :]), zf_done.sem)
                    dve.wait_ge(zhi_done.sem, zhi_done.done(u))
                    dst = (slice(None), u % KD, slice((u // KD) * HALF, (u // KD + 1) * HALF))
                    link(dve.tensor_tensor(ylo[dst], gs[:, u % 2], yhi[dst].bitcast(F32), ALU.subtract), zlo_done)
                dve.wait_ge(gate1_in, 16)
                for j in range(2):
                    dve.wait_ge(wohi, 2 * (j + 1))
                    for q in range(2):
                        link(dve.tensor_tensor(wlo[:, q], wo[:, q], whi[:, q].bitcast(F32), ALU.subtract), wolo)
                    for t in range(TT):
                        u = j * TT + t
                        dve.wait_ge(m_mm, u + 1)
                        dve.wait_ge(xt_in[u % 2], 16 * (u // 2 + 1))
                        link(dve.tensor_tensor(pr[:, u % 2], acc[u % 4][:, :], gate1[:, j * HALF:(j + 1) * HALF], ALU.mult), m_read)
                        link(dve.tensor_tensor(xt[:, u % 2], xt[:, u % 2], pr[:, u % 2], ALU.add), m_done)

            @block.tensor
            def _(pe):
                for u in range(2 * KD):
                    k, g = u % KD, u // KD
                    pe.wait_ge(zf_done.sem, zf_done.free(u))
                    for t in range(4):
                        last = pe.transpose(pt[u % 2][:, t * P:(t + 1) * P], z[:, 4 * g + t, k * P:(k + 1) * P], K.ident[:, :])
                    last.then_inc(zt_mm.sem, 1)
                pe.wait_ge(zlo_done, 2 * KD)
                for u, (j, t) in enumerate(units):
                    pe.wait_ge(wolo, 2 * (j + 1))
                    if u >= 4:
                        pe.wait_ge(m_read, u - 3)
                    for k in range(KD):
                        last = three_pass(pe, acc[u % 4][:, :], yhi[:, k, t * P:(t + 1) * P], ylo[:, k, t * P:(t + 1) * P],
                                          whi[:, k // 4, k % 4], wlo[:, k // 4, k % 4], k, KD)
                    last.then_inc(m_mm, 1)


HC = 2 * HEADS
NBEST = TOPK * TOPK


def route_phase(nc, h2hi, h2lo, w_query, sub_keys, iT, jT, wT, keep):
    K = keep
    with ExitStack() as ctx:
        sem = ctx.enter_context(phase_semaphores(nc))
        sb = lambda n, s, d=F32: ctx.enter_context(nc.sbuf_tensor(n, s, d))
        w = sb("qw_raw", [P, 2, KD, P])
        whi, wlo = sb("qwhi", [P, 2, KD, P], F32R), sb("qwlo", [P, 2, KD, P], F32R)
        kraw, kT = sb("kraw", [P, 2, P]), sb("keysT", [P, 2, P])
        qT = sb("rqT", [P, 2, T])
        s = sb("rs", [P, 2, TT, NKEYS])
        s2 = sb("rs2", [P, 2, NKEYS])
        tv, tix, tf = sb("rtv", [P, TT, TOPK]), sb("rti", [P, TT, TOPK], U32), sb("rtf", [P, TT, TOPK])
        TV, TI = sb("TV", [P, TT, HC, TOPK]), sb("TI", [P, TT, HC, TOPK])
        pq = [ctx.enter_context(nc.psum_tensor(f"rpq{i}", [P, HALF], F32)) for i in range(2)]
        pk = ctx.enter_context(nc.psum_tensor("rpk", [P, P], F32))
        psc = [ctx.enter_context(nc.psum_tensor(f"rps{i}", [P, 4, NKEYS], F32)) for i in range(2)]
        w_in, k_in = [sem(f"rw_in{i}") for i in range(2)], [sem(f"rk_in{i}") for i in range(2)]
        hi_done, lo_done = Steps(sem("rhi_done"), 2), Steps(sem("rlo_done"), 2)
        q_mm, q_cp = Steps(sem("rq_mm"), 2), Steps(sem("rq_cp"), 2)
        k_mm, k_cp = Steps(sem("rk_mm"), 2), Steps(sem("rk_cp"), 1)
        s_mm, s_cp = Steps(sem("rs_mm"), 2), Steps(sem("rs_cp"), 2)
        top_done = Steps(sem("rtop_done"), 2)
        settled = sem("r_settled")
        wv = w_query.rearrange("(k p) n -> p k n", p=P)
        kv = sub_keys.rearrange("h c k d -> (h c) k d")
        with nc.Block() as block:
            @block.sync
            def _(sp):
                for steps in (hi_done, lo_done, q_mm, q_cp, k_mm, k_cp, s_mm, s_cp, top_done):
                    steps.open(sp)
                with sp.Fori(0, HC // 2) as turn:
                    for p in range(2):
                        c = turn * 2 + p
                        sp.wait_ge(lo_done.sem, lo_done.free(c))
                        sp.dma_start(w[:, p], wv[:, :, bass.ds(c * P, P)]).then_inc(w_in[p], 16)
                        sp.wait_ge(k_mm.sem, k_mm.free(c))
                        sp.dma_start(kraw[:, p], kv[bass.ds(c, 1)].rearrange("o k d -> (o k) d")).then_inc(k_in[p], 16)

            @block.scalar
            def _(act):
                with act.Fori(0, HC // 2) as turn:
                    for p in range(2):
                        c = turn * 2 + p
                        act.wait_ge(w_in[p], turn * 16 + 16)
                        act.wait_ge(k_cp.sem, k_cp.free(c))
                        act.activation(whi[:, p], w[:, p], ACT.Copy).then_inc(hi_done.sem, 1)
                        act.wait_ge(k_mm.sem, k_mm.done(c))
                        act.activation(kT[:, p], pk[:, :], ACT.Copy).then_inc(k_cp.sem, 1)
                        for h in range(2):
                            act.wait_ge(q_mm.sem, q_mm.done(c * 2 + h))
                            act.activation(qT[:, p, h * HALF:(h + 1) * HALF], pq[h][:, :], ACT.Copy).then_inc(q_cp.sem, 1)
                        act.wait_ge(top_done.sem, top_done.free(c))
                        for h in range(2):
                            act.wait_ge(s_mm.sem, s_mm.done(c * 2 + h))
                            act.activation(s[:, p, 4 * h:4 * h + 4], psc[h][:, :, :], ACT.Copy).then_inc(s_cp.sem, 1)

            @block.vector
            def _(dve):
                link = Chain(dve, sem("dve_route"))

                def cut_low(c, p):
                    dve.wait_ge(hi_done.sem, hi_done.done(c))
                    link(dve.tensor_tensor(wlo[:, p], w[:, p], whi[:, p].bitcast(F32), ALU.subtract), lo_done.sem)

                def search(c, p):
                    for t in range(TT):
                        if t % 4 == 0:
                            dve.wait_ge(s_cp.sem, s_cp.done(c * 2 + t // 4))
                        x, y = s[:, p, t], s2[:, t % 2]
                        settle(dve, settled)
                        link(dve.max(tv[:, t, 0:8], x))
                        settle(dve, settled)
                        link(dve.max_index(tix[:, t, 0:8], tv[:, t, 0:8], x))
                        settle(dve, settled)
                        link(dve.match_replace(y, tv[:, t, 0:8], x, NEG))
                        settle(dve, settled)
                        link(dve.max(tv[:, t, 8:16], y))
                        settle(dve, settled)
                        link(dve.max_index(tix[:, t, 8:16], tv[:, t, 8:16], y))
                    dve.sem_inc(top_done.sem, 1)
                    link(dve.tensor_copy(TV[:, :, bass.ds(c, 1), :].rearrange("p t o k -> p t (o k)"), tv[:, :, :]))
                    link(dve.tensor_copy(TI[:, :, bass.ds(c, 1), :].rearrange("p t o k -> p t (o k)"), tix[:, :, :]))

                cut_low(0, 0)
                with dve.Fori(0, HC // 2 - 1) as turn:
                    link.enter(turn, 2 * (1 + 5 * TT + 2))
                    for p in range(2):
                        cut_low(turn * 2 + (p + 1), 1 - p)
                        search(turn * 2 + p, p)
                link.leave(HC // 2 - 1)
                cut_low(HC - 1, 1)
                search(HC - 2, 0)
                search(HC - 1, 1)

            @block.tensor
            def _(pe):
                with pe.Fori(0, HC // 2) as turn:
                    for p in range(2):
                        c = turn * 2 + p
                        pe.wait_ge(k_in[p], turn * 16 + 16)
                        pe.wait_ge(k_cp.sem, k_cp.free(c))
                        pe.transpose(pk[:, :], kraw[:, p], K.ident[:, :]).then_inc(k_mm.sem, 1)
                        pe.wait_ge(lo_done.sem, lo_done.done(c))
                        for h in range(2):
                            pe.wait_ge(q_cp.sem, q_cp.free(c * 2 + h))
                            for k in range(KD):
                                last = three_pass(pe, pq[h][:, :], whi[:, p, k], wlo[:, p, k],
                                                  h2hi[:, k, h * HALF:(h + 1) * HALF], h2lo[:, k, h * HALF:(h + 1) * HALF], k, KD)
                            last.then_inc(q_mm.sem, 1)
                        for h in range(2):
                            pe.wait_ge(q_cp.sem, q_cp.done(c * 2 + h))
                            pe.wait_ge(k_cp.sem, k_cp.done(c))
                            pe.wait_ge(s_cp.sem, s_cp.free(c * 2 + h))
                            for t in range(4):
                                last = pe.matmul(psc[h][:, t], qT[:, p, (4 * h + t) * P:(4 * h + t + 1) * P], kT[:, p], start=True, stop=True)
                            last.then_inc(s_mm.sem, 1)

        cand = sb("cand", [P, HEADS, NBEST])
        cand2 = sb("cand2", [P, NBEST])
        best, bj = sb("best", [P, HEADS, TOPK]), sb("bj", [P, HEADS, TOPK], U32)
        code = sb("code", [P, 2, HEADS * TOPK], U32)
        rank = sb("rank", [P, 2, HEADS * TOPK])
        eq = sb("eq", [P, HEADS, TOPK, TOPK])
        den = sb("rden", [P, HEADS])
        pick = sb("pick", [P, 3, HEADS * TOPK])
        pt = ctx.enter_context(nc.psum_tensor("rpt", [P, 3, P], F32))
        pick_done, pick_mm, pick_cp, bm_done, be_done = (sem(n) for n in ("pick_done", "pick_mm", "pick_cp", "bm_done", "be_done"))
        with nc.Block() as block:
            @block.scalar
            def _(act):
                with act.Fori(0, TT) as t:
                    act.wait_ge(bm_done, t + 1)
                    act.activation(best[:, :, :], best[:, :, :], ACT.Exp).then_inc(be_done, 1)

            @block.vector
            def _(dve):
                link = Chain(dve, sem("dve_best"))
                with dve.Fori(0, TT) as t:
                    link.enter(t, PER_BEST)
                    tl = lambda X: X[:, bass.ds(t, 1)].rearrange("p o (h c) k -> p (o h) c k", c=2)
                    va, vb = tl(TV)[:, :, 0], tl(TV)[:, :, 1]
                    link(dve.tensor_tensor(cand[:, :, :].rearrange("p h (a b) -> p h a b", b=TOPK),
                                           va[:, :, :, None].to_broadcast([P, HEADS, TOPK, TOPK]),
                                           vb[:, :, None, :].to_broadcast([P, HEADS, TOPK, TOPK]), ALU.add))
                    for h in range(HEADS):
                        x, y = cand[:, h], cand2[:, :]
                        settle(dve, settled)
                        link(dve.max(best[:, h, 0:8], x))
                        settle(dve, settled)
                        link(dve.max_index(bj[:, h, 0:8], best[:, h, 0:8], x))
                        settle(dve, settled)
                        link(dve.match_replace(y, best[:, h, 0:8], x, NEG))
                        settle(dve, settled)
                        link(dve.max(best[:, h, 8:16], y))
                        settle(dve, settled)
                        link(dve.max_index(bj[:, h, 8:16], best[:, h, 8:16], y))
                    link(dve.tensor_copy(den[:, :], best[:, :, 0]))
                    link(dve.tensor_tensor(best[:, :, :], best[:, :, :], den[:, :, None].to_broadcast([P, HEADS, TOPK]), ALU.subtract), bm_done)
                    bf = bj[:, :, :].rearrange("p h k -> p (h k)")
                    link(dve.tensor_single_scalar(code[:, 0], bf, 4, ALU.logical_shift_right))
                    link(dve.tensor_single_scalar(code[:, 1], bf, 15, ALU.bitwise_and))
                    link(dve.tensor_copy(rank[:, :, :], code[:, :, :]))
                    for c in range(2):
                        link(dve.tensor_tensor(eq[:, :, :, :].rearrange("p h k a -> p (h k) a"),
                                               rank[:, c, :, None].to_broadcast([P, HEADS * TOPK, TOPK]),
                                               K.iota[:, None, 0:TOPK].to_broadcast([P, HEADS * TOPK, TOPK]), ALU.is_equal))
                        link(dve.tensor_tensor(eq[:, :, :, :], eq[:, :, :, :],
                                               tl(TI)[:, :, c, None, :].to_broadcast([P, HEADS, TOPK, TOPK]), ALU.mult))
                        if c == 0:
                            dve.wait_ge(be_done, t + 1)
                        link(dve.tensor_reduce(pick[:, c], eq[:, :, :, :].rearrange("p h k a -> p (h k) a"), AX, ALU.add))
                    link(dve.tensor_reduce(den[:, :], best[:, :, :], AX, ALU.add))
                    link(dve.reciprocal(den[:, :], den[:, :]))
                    link(dve.tensor_tensor(pick[:, 2].rearrange("p (h k) -> p h k", h=HEADS), best[:, :, :],
                                           den[:, :, None].to_broadcast([P, HEADS, TOPK]), ALU.mult), pick_done)
                    dve.wait_ge(pick_mm, t + 1)
                    for c, dst in enumerate((iT, jT, wT)):
                        link(dve.tensor_copy(dst[:, bass.ds(t * P, P)], pt[:, c]), *[pick_cp] * (c == 2))
                link.leave(TT)

            @block.tensor
            def _(pe):
                with pe.Fori(0, TT) as t:
                    pe.wait_ge(pick_done, t + 1)
                    for c in range(3):
                        last = pe.transpose(pt[:, c], pick[:, c], K.ident[:, :])
                    last.then_inc(pick_mm, 1)


PER_BEST = 1 + 5 * HEADS + 2 + 3 + 6 + 3 + 3


def gate_phase(nc, iT, jT, wT, gates, keep):
    K = keep
    BT = 64
    G = 4
    NG = BT // G
    with ExitStack() as ctx:
        sem = ctx.enter_context(phase_semaphores(nc))
        sb = lambda n, s, d=F32: ctx.enter_context(nc.sbuf_tensor(n, s, d))
        col = sb("gcol", [P, 2 * G, P])
        row = sb("grow", [P, 2 * G, P])
        stage = sb("gstage", [P, P, 2 * BT])
        pg = [ctx.enter_context(nc.psum_tensor(f"gp{i}", [P, G, P], F32)) for i in range(2)]
        hot_done, g_mm, g_cp = Steps(sem("hot_done"), 2), Steps(sem("g_mm"), 2), Steps(sem("g_cp"), 2)
        st_out = [Steps(sem(f"st_out{i}"), 1, 16) for i in range(2)]
        TURNS = T // (2 * G)
        gv = gates.rearrange("i j t -> j i t")
        with nc.Block() as block:
            @block.vector
            def _(dve):
                for steps in (hot_done, g_mm, g_cp, *st_out):
                    steps.open(dve)
                with dve.Fori(0, TURNS) as turn:
                    for u in range(2):
                        dve.wait_ge(g_mm.sem, g_mm.free(turn * 2 + u))
                        for q in range(G):
                            at = bass.ds(turn * (2 * G) + (u * G + q), 1)
                            dve.tensor_scalar(col[:, u * G + q], K.iota[:, :], jT[:, at], None, ALU.is_equal)
                            last = dve.tensor_scalar(row[:, u * G + q], K.iota[:, :], iT[:, at], wT[:, at], ALU.is_equal, ALU.mult)
                        last.then_inc(hot_done.sem, 1)

            @block.tensor
            def _(pe):
                with pe.Fori(0, TURNS) as turn:
                    for u in range(2):
                        pe.wait_ge(hot_done.sem, hot_done.done(turn * 2 + u))
                        pe.wait_ge(g_cp.sem, g_cp.free(turn * 2 + u))
                        for q in range(G):
                            last = pe.matmul(pg[u][:, q], col[:, u * G + q], row[:, u * G + q], start=True, stop=True)
                        last.then_inc(g_mm.sem, 1)

            @block.scalar
            def _(act):
                with act.Fori(0, T // (2 * BT)) as blk:
                    for half in range(2):
                        act.wait_ge(st_out[half].sem, st_out[half].free(blk))
                        with act.Fori(0, NG // 2) as pair:
                            for u in range(2):
                                n = (blk * 2 + half) * NG + (pair * 2 + u)
                                act.wait_ge(g_mm.sem, g_mm.done(n))
                                act.activation(stage[:, :, bass.ds(pair * (2 * G) + (half * BT + u * G), G)].rearrange("p i t -> p t i"),
                                               pg[u][:, :, :], ACT.Copy).then_inc(g_cp.sem, 1)

            @block.sync
            def _(sp):
                with sp.Fori(0, T // (2 * BT)) as blk:
                    for half in range(2):
                        sp.wait_ge(g_cp.sem, g_cp.done((blk * 2 + half) * NG + (NG - 1)))
                        sp.dma_start(gv[:, :, bass.ds(blk * (2 * BT) + half * BT, BT)],
                                     stage[:, :, half * BT:(half + 1) * BT]).then_inc(st_out[half].sem, 16)
                for half in range(2):
                    sp.wait_ge(st_out[half].sem, st_out[half].done(T // (2 * BT) - 1))


def expert_phase(nc, h2hi, h2lo, expert_u, expert_v, gates, acc, keep):
    K = keep
    Q = 4
    GROUPS = NKEYS // Q
    with ExitStack() as ctx:
        sem = ctx.enter_context(phase_semaphores(nc))
        sb = lambda n, s, d=F32: ctx.enter_context(nc.sbuf_tensor(n, s, d))
        ur, vr, gr = sb("ur", [P, 2, D]), sb("vraw", [P, D]), sb("gr", [P, 2, T])
        uhi, ulo = sb("uhi", [P, 2, KD, P], F32R), sb("ulo", [P, 2, KD, P], F32R)
        vhi, vlo = sb("vhi", [P, Q, D], F32R), sb("vlo", [P, Q, D], F32R)
        Hhi, Hlo = sb("Hhi", [P, Q, T], F32R), sb("Hlo", [P, Q, T], F32R)
        ge = sb("ge", [P, 2, HALF])
        tb, pa = ([ctx.enter_context(nc.psum_tensor(f"{n}{i}", [P, HALF], F32)) for i in range(2)] for n in ("etb", "epa"))
        vo = [ctx.enter_context(nc.psum_tensor(f"evo{i}", [P, HALF], F32)) for i in range(4)]
        u_in, g_in = [sem(f"u_in{i}") for i in range(2)], [sem(f"g_in{i}") for i in range(2)]
        v_in = sem("v_in")
        ut_mm, uhi_done, ulo_done = (Steps(sem(n), 2) for n in ("ut_mm", "uhi_done", "ulo_done"))
        ut_rows = Steps(sem("ut_rows"), 2)
        vhi_done, vlo_done = Steps(sem("vhi_done"), 1), Steps(sem("vlo_done"), 1)
        a_mm, ge_done, H_done, Hhi_done, Hlo_done = (Steps(sem(n), 2) for n in ("a_mm", "ge_done", "H_done", "Hhi_done", "Hlo_done"))
        g_free = Steps(sem("g_free"), 2)
        vo_mm, vo_add = Steps(sem("vo_mm"), 4), Steps(sem("vo_add"), 4)
        UNITS = 2 * TT
        with nc.Block() as block:
            @block.sync
            def _(sp):
                for steps in (ut_mm, ut_rows, uhi_done, ulo_done, vhi_done, vlo_done, a_mm, ge_done, H_done, Hhi_done, Hlo_done, g_free, vo_mm, vo_add):
                    steps.open(sp)
                with sp.Fori(0, NKEYS // 2) as turn:
                    for p in range(2):
                        n = turn * 2 + p
                        sp.wait_ge(ut_rows.sem, ut_rows.free(n))
                        sp.dma_start(ur[:, p], expert_u[bass.ds(n * P, P), :]).then_inc(u_in[p], 16)
                        sp.wait_ge(vlo_done.sem, vlo_done.free(n))
                        sp.dma_start(vr[:, :], expert_v[bass.ds(n * P, P), :]).then_inc(v_in, 16)

            @block.gpsimd
            def _(pool):
                with pool.Fori(0, NKEYS // 2) as turn:
                    for p in range(2):
                        n = turn * 2 + p
                        pool.wait_ge(g_free.sem, g_free.free(n))
                        pool.dma_start(gr[:, p], gates[bass.ds(n, 1)].rearrange("o j t -> (o j) t")).then_inc(g_in[p], 16)

            @block.scalar
            def _(act):
                link = Chain(act, sem("act_experts"))

                def cut_u(n, p):
                    for c in range(2):
                        act.wait_ge(ut_mm.sem, ut_mm.done(n * 2 + c))
                        link(act.activation(uhi[:, p, 4 * c:4 * c + 4], tb[c][:, :].rearrange("p (k e) -> p k e", k=4), ACT.Copy), uhi_done.sem)

                def group(g, last):
                    for q in range(Q):
                        n = g * Q + q
                        p = q % 2
                        if not (last and q == Q - 1):
                            cut_u(n + 1, 1 - p)
                        act.wait_ge(v_in, n * 16 + 16)
                        act.wait_ge(vo_mm.sem, vo_mm.free(g * UNITS + 3))
                        link(act.activation(vhi[:, q], vr[:, :], ACT.Copy), vhi_done.sem)
                        for h in range(2):
                            act.wait_ge(a_mm.sem, a_mm.done(n * 2 + h))
                            link(act.activation(ge[:, h], pa[h][:, :], ACT.Gelu), ge_done.sem)
                            act.wait_ge(H_done.sem, H_done.done(n * 2 + h))
                            link(act.activation(Hhi[:, q, h * HALF:(h + 1) * HALF], gr[:, p, h * HALF:(h + 1) * HALF], ACT.Copy), Hhi_done.sem)

                cut_u(0, 0)
                with act.Fori(0, GROUPS - 1) as g:
                    link.enter(g, Q * 7)
                    group(g, False)
                link.leave(GROUPS - 1)
                group(GROUPS - 1, True)

            @block.vector
            def _(dve):
                link = Chain(dve, sem("dve_experts"))

                def cut_u(n, p):
                    for c in range(2):
                        dve.wait_ge(uhi_done.sem, uhi_done.done(n * 2 + c))
                        link(dve.tensor_tensor(ulo[:, p, 4 * c:4 * c + 4], tb[c][:, :].rearrange("p (k e) -> p k e", k=4),
                                               uhi[:, p, 4 * c:4 * c + 4].bitcast(F32), ALU.subtract), ulo_done.sem, *[ut_rows.sem] * c)

                def group(g, last):
                    for q in range(Q):
                        n = g * Q + q
                        p = q % 2
                        if not (last and q == Q - 1):
                            cut_u(n + 1, 1 - p)
                        dve.wait_ge(vhi_done.sem, vhi_done.done(n))
                        link(dve.tensor_tensor(vlo[:, q], vr[:, :], vhi[:, q].bitcast(F32), ALU.subtract), vlo_done.sem)
                        dve.wait_ge(g_in[p], (g * 32 + (q // 2) * 16) + 16)
                        for h in range(2):
                            hs = slice(h * HALF, (h + 1) * HALF)
                            dve.wait_ge(ge_done.sem, ge_done.done(n * 2 + h))
                            link(dve.tensor_tensor(gr[:, p, hs], gr[:, p, hs], ge[:, h], ALU.mult), H_done.sem)
                            dve.wait_ge(Hhi_done.sem, Hhi_done.done(n * 2 + h))
                            link(dve.tensor_tensor(Hlo[:, q, hs], gr[:, p, hs], Hhi[:, q, hs].bitcast(F32), ALU.subtract),
                                 Hlo_done.sem, *[g_free.sem] * h)
                    for u in range(UNITS):
                        dve.wait_ge(vo_mm.sem, vo_mm.done(g * UNITS + u))
                        at = acc[:, u // 2, (u % 2) * HALF:(u % 2 + 1) * HALF]
                        link(dve.tensor_tensor(at, at, vo[u % 4][:, :], ALU.add), vo_add.sem)

                link(dve.memset(acc[:, :, :], 0.0))
                cut_u(0, 0)
                with dve.Fori(0, GROUPS - 1) as g:
                    link.enter(g, Q * 7 + UNITS)
                    group(g, False)
                link.leave(GROUPS - 1)
                group(GROUPS - 1, True)

            @block.tensor
            def _(pe):
                def turn_u(n, p, at):
                    pe.wait_ge(u_in[p], at)
                    for c in range(2):
                        pe.wait_ge(ulo_done.sem, ulo_done.free(n * 2 + c))
                        for k in range(4):
                            last = pe.transpose(tb[c][:, k * P:(k + 1) * P], ur[:, p, (4 * c + k) * P:(4 * c + k + 1) * P], K.ident[:, :])
                        last.then_inc(ut_mm.sem, 1)

                def group(g, last):
                    for q in range(Q):
                        n = g * Q + q
                        p = q % 2
                        if not (last and q == Q - 1):
                            turn_u(n + 1, 1 - p, g * 32 + ((q + 1) // 2 * 16 + 16))
                        pe.wait_ge(ulo_done.sem, ulo_done.done(n * 2 + 1))
                        for h in range(2):
                            pe.wait_ge(ge_done.sem, ge_done.free(n * 2 + h))
                            for k in range(KD):
                                step = three_pass(pe, pa[h][:, :], uhi[:, p, k], ulo[:, p, k], h2hi[:, k, h * HALF:(h + 1) * HALF],
                                                  h2lo[:, k, h * HALF:(h + 1) * HALF], k, KD)
                            step.then_inc(a_mm.sem, 1)
                    for u in range(UNITS):
                        t, dh = u // 2, u % 2
                        if u in (0, UNITS // 2):
                            pe.wait_ge(Hlo_done.sem, Hlo_done.done((g * Q + (Q - 1)) * 2 + u // (UNITS // 2)))
                        pe.wait_ge(vo_add.sem, vo_add.free(g * UNITS + u))
                        for q in range(Q):
                            step = three_pass(pe, vo[u % 4][:, :], Hhi[:, q, t * P:(t + 1) * P], Hlo[:, q, t * P:(t + 1) * P],
                                              vhi[:, q, dh * HALF:(dh + 1) * HALF], vlo[:, q, dh * HALF:(dh + 1) * HALF], q, Q)
                        step.then_inc(vo_mm.sem, 1)

                turn_u(0, 0, 16)
                with pe.Fori(0, GROUPS - 1) as g:
                    group(g, False)
                group(GROUPS - 1, True)


def finish_phase(nc, acc, x1, gate2_dram, out):
    with ExitStack() as ctx:
        sem = ctx.enter_context(phase_semaphores(nc))
        sb = lambda n, s, d=F32: ctx.enter_context(nc.sbuf_tensor(n, s, d))
        gate = sb("gate2", [P, D])
        xt = sb("fx", [P, TT, D])
        f_in, f_done, f_out = [sem(f"f_in{i}") for i in range(2)], sem("f_done"), sem("f_out")
        with nc.Block() as block:
            @block.sync
            def _(sp):
                sp.dma_start(gate[:, :], gate2_dram.to_broadcast([P, D])).then_inc(f_in[0], 16)
                sp.dma_start(xt[:, :, :], x1.rearrange("(t p) d -> p t d", p=P)).then_inc(f_in[1], 16)
                for t in range(TT):
                    sp.wait_ge(f_done, t + 1)
                    sp.dma_start(out[t * P:(t + 1) * P, :], xt[:, t]).then_inc(f_out, 16)
                sp.wait_ge(f_out, 16 * TT)

            @block.vector
            def _(dve):
                link = Chain(dve, sem("dve_finish"))
                for s in f_in:
                    dve.wait_ge(s, 16)
                for t in range(TT):
                    link(dve.tensor_tensor(acc[:, t], acc[:, t], gate[:, :], ALU.mult))
                    link(dve.tensor_tensor(xt[:, t], xt[:, t], acc[:, t], ALU.add), f_done)


def dump(nc, out, src, sem):
    o_done = sem("o_done")
    with nc.Block() as block:
        @block.sync
        def _(sp):
            sp.dma_start(out, src).then_inc(o_done, 16)
            sp.wait_ge(o_done, 16)


class Keep:
    pass


def program(nc, io, out, upto=99):
    dram = lambda n, s: nc.dram_tensor(n, s, F32, kind="Internal").ap()
    io["mod_dram"] = dram("mod_dram", [N_MOD * D])
    proj = dram("proj_dram", [T, D_IN])
    x1 = dram("x1_dram", [T, D])
    gates = dram("gates_dram", [NKEYS, NKEYS, T])
    K = Keep()
    with ExitStack() as ctx:
        sb = lambda n, s, d=F32: ctx.enter_context(nc.sbuf_tensor(n, s, d))
        sem = lambda n: ctx.enter_context(nc.semaphore(n))
        K.ident, K.identr = sb("ident", [P, P]), sb("identr", [P, P], F32R)
        K.iota = sb("iota", [P, P])
        K.par = sb("par", [P, 80])
        K.mod = sb("mod", [P, 6 * KD])
        K.a1, K.a2 = sb("a1", [P, KD]), sb("a2", [P, KD])
        K.lbd, K.lbs = sb("lbd", [P, NH]), sb("lbs", [P, NH])
        K.eps = sb("eps", [P, 1])
        K.hgw, K.qw, K.kw, K.sink = sb("hgw", [P, P]), sb("qw", [P, HD]), sb("kw", [P, HD]), sb("sink", [P, SWH])
        setup_phase(nc, io, K)
        with ExitStack() as c2:
            hhi = c2.enter_context(nc.sbuf_tensor("hhi", [P, KD, T], F32R))
            hlo = c2.enter_context(nc.sbuf_tensor("hlo", [P, KD, T], F32R))
            norm_phase(nc, "1", io["x"][0], K.a1, K.mod[:, 0:8], hhi, hlo, K)
            W = D_IN // 16
            token_gemm_phase(nc, "i", hhi, hlo, KD, io["w_in"][0].rearrange("(k p) n -> p k n", p=P), W, 16, proj)
        if upto == 1:
            o_done = sem("o_done")
            with nc.Block() as block:
                @block.sync
                def _(sp):
                    sp.dma_start(out[0], proj[:, DEBUG_COL:DEBUG_COL + D]).then_inc(o_done, 16)
                    sp.wait_ge(o_done, 16)
            return
        with ExitStack() as c2:
            yhi = c2.enter_context(nc.sbuf_tensor("yhi", [P, KD, T], F32R))
            ylo = c2.enter_context(nc.sbuf_tensor("ylo", [P, KD, T], F32R))
            mixer_phase(nc, proj, yhi, ylo, K)
            merge_phase(nc, yhi, ylo, proj, io["w_branch"], io["w_out"], io["x"][0],
                        io["mod_dram"][None, 2 * D:3 * D], x1, K)
        if upto == 3:
            dump(nc, out[0], x1, sem)
            return
        acc = sb("acc", [P, TT, D])
        h2hi, h2lo = sb("h2hi", [P, KD, T], F32R), sb("h2lo", [P, KD, T], F32R)
        norm_phase(nc, "2", x1, K.a2, K.mod[:, 24:32], h2hi, h2lo, K)
        with ExitStack() as c2:
            iT, jT, wT = (c2.enter_context(nc.sbuf_tensor(n, [P, T], F32)) for n in ("iT", "jT", "wT"))
            route_phase(nc, h2hi, h2lo, io["w_query"][0], io["sub_keys"][0], iT, jT, wT, K)
            gate_phase(nc, iT, jT, wT, gates, K)
        expert_phase(nc, h2hi, h2lo, io["expert_u"][0], io["expert_v"][0], gates, acc, K)
        finish_phase(nc, acc, x1, io["mod_dram"][None, 5 * D:6 * D], out[0])


DEBUG_COL = 0
_INS = ["x", "c", "w_ada", "b_ada", "norm_mix_w", "w_in", "hg_lb_raw", "hg_norm_w", "q_norm_w", "k_norm_w", "sinks",
        "w_branch", "w_out", "norm_ffn_w", "w_query", "sub_keys", "expert_u", "expert_v"]


def kernel(**inputs):
    import concourse.bacc as _bacc
    from concourse.bass_utils import run_bass_kernel_spmd as _run

    nc = _bacc.Bacc("TRN2", target_bir_lowering=False, num_devices=1)
    arrays, io = {}, {}
    for name in _INS:
        a = np.ascontiguousarray(inputs[name])
        arrays[f"in_{name}"] = a
        io[name] = nc.dram_tensor(f"in_{name}", a.shape, mybir.dt.from_np(a.dtype), kind="ExternalInput").ap()
    out = nc.dram_tensor("out_0", (1, T, D), F32, kind="ExternalOutput").ap()
    program(nc, io, out)
    r = _run(nc, [arrays], core_ids=[0])
    return r.results[0]["out_0"]
```

```python
import numpy as np
import concourse.bass as bass
from concourse import mybir
from contextlib import ExitStack, contextmanager

F32 = mybir.dt.float32
F32R = mybir.dt.float32r
I32 = mybir.dt.int32
U32 = mybir.dt.uint32
ALU = mybir.AluOpType
ACT = mybir.ActivationFunctionType
AX = mybir.AxisListType.X

P = 128
D = 1024
T = 1024
KD = D // P
TT = T // P
HALF = 512
D_IN = 4864
COL_HQ, COL_HF, COL_HI, COL_HG, COL_SQ, COL_SK, COL_SV, COL_GL = 0, 512, 1024, 1536, 2048, 2560, 2688, 2816
N_MOD = 6
EPS = 1e-6
NH = 4
SWH, SWKV, HD = 8, 2, 64
HEADS, TOPK, NKEYS = 8, 16, 128
NEG = -1e30

class Chain:

    def __init__(self, eng, sem):
        self.eng, self.sem, self.start, self.n, self.base = eng, sem, 0, 0, 0

    def __call__(self, ins, *signals):
        self.n += 1
        ins.then_inc(self.sem, 1)
        self.eng.wait_ge(self.sem, self.base + self.n)
        for s in signals:
            self.eng.sem_inc(s, 1)

    def together(self, steps, *signals):
        for ins in steps[:-1]:
            self.n += 1
            ins.then_inc(self.sem, 1)
        self(steps[-1], *signals)

    def enter(self, turn, per):
        self.start += self.n
        self.base, self.n, self.per = self.start + turn * per, 0, per

    def leave(self, turns):
        assert self.n == self.per, (self.n, self.per)
        self.start += self.per * turns
        self.base, self.n = self.start, 0

class Steps:

    def __init__(self, sem, slots, unit=1):
        self.sem, self.slots, self.unit = sem, slots, unit

    def open(self, eng):
        eng.sem_inc(self.sem, self.slots * self.unit)

    def done(self, n):
        return n * self.unit + (self.slots + 1) * self.unit

    def free(self, n):
        return n * self.unit + self.unit

class Soft:

    def __init__(self, sem):
        self.sem, self.base, self.issued = sem, 0, 0

    def start(self, dmas):
        self.base, self.issued = self.base + self.issued, 16 * dmas
        return self

    def value(self, arrived):
        return arrived + self.base

def settle(eng, sem):
    eng.sem_inc(sem, 1)

@contextmanager
def phase_semaphores(nc):
    with ExitStack() as ctx:
        taken = []

        def sem(name):
            taken.append(ctx.enter_context(nc.semaphore(name)))
            return taken[-1]

        yield sem
        with nc.Block() as block:
            @block.gpsimd
            def _(pool):
                for one in taken:
                    pool.sem_clear(one)

def setup_phase(nc, io, keep):
    NB = N_MOD * D // HALF
    NLOAD = 8
    with ExitStack() as ctx:
        sem = ctx.enter_context(phase_semaphores(nc))
        sb = lambda n, s, d=F32: ctx.enter_context(nc.sbuf_tensor(n, s, d))
        ps = lambda n, s: ctx.enter_context(nc.psum_tensor(n, s, F32))
        prow = sb("prow", [P, P])
        wada = sb("wada", [P, 4, KD, HALF])
        csig = sb("csig", [P, KD])
        cact = sb("cact", [P, KD])
        modr, bada = sb("modr", [1, N_MOD * D]), sb("bada", [1, N_MOD * D])
        modt = sb("modt", [6 * KD, P])
        pp = ps("pp", [P, P])
        pm = [ps(f"pm{i}", [1, HALF]) for i in range(4)]
        pt = ps("pt", [P, 6 * KD])
        par_in, wada_in = sem("par_in"), [sem(f"wada_in{i}") for i in range(4)]
        id_done, par_t, par_cp, sig_done = sem("id_done"), sem("par_t"), sem("par_cp"), sem("sig_done")
        cact_done, mod_mm, mod_add = sem("cact_done"), Steps(sem("mod_mm"), 4), Steps(sem("mod_add"), 4)
        modT_t, mod_st, modt_in, bada_in = sem("modT_t"), sem("mod_st"), sem("modt_in"), sem("bada_in")
        lbd_done = sem("lbd_done")
        K = keep
        NPAR = 8 + 8 + 8 + 8
        wv = io["w_ada"][0].rearrange("(k p) n -> p k n", p=P)

        def load_half(eng, half):
            ks = slice(half * KD // 2, (half + 1) * KD // 2)
            with eng.Fori(0, NB // 4) as turn:
                for s in range(4):
                    b = turn * 4 + s
                    eng.wait_ge(mod_mm.sem, mod_mm.free(b))
                    eng.dma_start(wada[:, s, ks], wv[:, ks, bass.ds(b * HALF, HALF)]).then_inc(wada_in[s], 16)

        with nc.Block() as block:
            @block.sync
            def _(sp):
                for steps in (mod_mm, mod_add):
                    steps.open(sp)
                rows = [(io["c"][0].rearrange("(a b) -> a b", b=P), 8),
                        (io["norm_mix_w"][0].rearrange("(a b) -> a b", b=P), 8),
                        (io["norm_ffn_w"][0].rearrange("(a b) -> a b", b=P), 8),
                        (io["hg_lb_raw"].rearrange("l (a b) -> (l a) b", b=P), 8)]
                at = 0
                for src, n in rows:
                    sp.dma_start(prow[at:at + n, :], src).then_inc(par_in, 16)
                    at += n
                sp.dma_start(K.hgw[:, :], io["hg_norm_w"][0:1, :].to_broadcast([P, P])).then_inc(par_in, 16)
                sp.dma_start(K.qw[:, :], io["q_norm_w"][0:1, :].to_broadcast([P, HD])).then_inc(par_in, 16)
                sp.dma_start(K.kw[:, :], io["k_norm_w"][0:1, :].to_broadcast([P, HD])).then_inc(par_in, 16)
                sp.dma_start(K.sink[:, :], io["sinks"][0:1, :].to_broadcast([P, SWH])).then_inc(par_in, 16)
                sp.dma_start(bada[:, :], io["b_ada"][0:1, :]).then_inc(bada_in, 16)
                load_half(sp, 0)
                sp.wait_ge(mod_add.sem, mod_add.done(NB - 1))
                sp.dma_start(io["mod_dram"][None, :], modr[:, :]).then_inc(mod_st, 16)
                sp.wait_ge(mod_st, 16)
                sp.dma_start(modt[:, :], io["mod_dram"].rearrange("(a b) -> a b", b=P)).then_inc(modt_in, 16)

            @block.gpsimd
            def _(pool):
                link = Chain(pool, sem("pool_setup"))
                link(pool.memset(K.ident[:, :], 0.0))
                link(pool.affine_select(out=K.ident[:, :], in_=K.ident[:, :], compare_op=ALU.not_equal, fill=1.0,
                                        base=0, pattern=[[-1, P]], channel_multiplier=1))
                pool.iota(K.iota[:, :], pattern=[[1, P]], base=0, channel_multiplier=0,
                          allow_small_or_imprecise_dtypes=True).then_inc(id_done, 1)

            @block.tensor
            def _(pe):
                pe.wait_ge(id_done, 1)
                pe.wait_ge(par_in, 16 * NLOAD)
                pe.transpose(pp[:, 0:NPAR], prow[0:NPAR, :], K.ident[0:NPAR, 0:NPAR]).then_inc(par_t, 1)
                pe.wait_ge(cact_done, 1)
                with pe.Fori(0, NB // 4) as turn:
                    b = turn * 4
                    for s in range(4):
                        pe.wait_ge(wada_in[s], b * 8 + 32)
                        pe.wait_ge(mod_add.sem, mod_add.free(b + s))
                        for k in range(KD):
                            last = pe.matmul(pm[s][:, :], cact[:, k:k + 1], wada[:, s, k], start=(k == 0), stop=(k == KD - 1))
                        last.then_inc(mod_mm.sem, 1)
                pe.wait_ge(modt_in, 16)
                pe.transpose(pt[:, :], modt[:, :], K.ident[0:6 * KD, 0:6 * KD]).then_inc(modT_t, 1)

            @block.scalar
            def _(act):
                act.wait_ge(par_cp, 1)
                act.activation(csig[:, :], K.par[:, 0:8], ACT.Sigmoid).then_inc(sig_done, 1)
                act.wait_ge(lbd_done, 1)
                act.activation(K.lbs[:, :], K.lbd[:, :], ACT.Sigmoid).then_inc(sig_done, 1)
                load_half(act, 1)

            @block.vector
            def _(dve):
                link = Chain(dve, sem("dve_setup"))
                dve.memset(K.eps[:, :], EPS)
                dve.wait_ge(par_t, 1)
                dve.tensor_copy(K.par[:, 0:NPAR], pp[:, 0:NPAR]).then_inc(par_cp, 1)
                dve.wait_ge(sig_done, 1)
                dve.tensor_tensor(cact[:, :], K.par[:, 0:8], csig[:, :], ALU.mult).then_inc(cact_done, 1)
                dve.tensor_tensor(K.lbd[:, :], K.par[:, 24:28], K.par[:, 28:32], ALU.subtract).then_inc(lbd_done, 1)
                dve.wait_ge(bada_in, 16)
                with dve.Fori(0, NB // 4) as turn:
                    b = turn * 4
                    for s in range(4):
                        dve.wait_ge(mod_mm.sem, mod_mm.done(b + s))
                        at = bass.ds((b + s) * HALF, HALF)
                        dve.tensor_tensor(modr[:, at], pm[s][:, :], bada[:, at], ALU.add).then_inc(mod_add.sem, 1)
                dve.wait_ge(modT_t, 1)
                link(dve.tensor_copy(K.mod[:, :], pt[:, :]))
                for w, sc, out in ((8, 8, K.a1), (16, 32, K.a2)):
                    link(dve.tensor_scalar(out[:, :], K.mod[:, sc:sc + 8], 1.0, None, ALU.add))
                    link(dve.tensor_tensor(out[:, :], out[:, :], K.par[:, w:w + 8], ALU.mult))

def norm_phase(nc, tag, src, a, shift, hhi, hlo, keep):
    K = keep
    with ExitStack() as ctx:
        sem = ctx.enter_context(phase_semaphores(nc))
        sb = lambda n, s, d=F32: ctx.enter_context(nc.sbuf_tensor(n + tag, s, d))
        x = sb("nx", [P, 4, D])
        sq = sb("nsq", [P, D])
        ssq = sb("nssq", [P, 4])
        rstd = sb("nrstd", [P, 4])
        hf = sb("nhf", [P, 2, HALF])
        pt = [ctx.enter_context(nc.psum_tensor(f"npt{tag}{i}", [P, HALF], F32)) for i in range(2)]
        x_in, ssq_done, root_done = [sem(f"x_in{t}" + tag) for t in range(4)], sem("ssq_done" + tag), sem("root_done" + tag)
        xs_done = Steps(sem("xs_done" + tag), 1)
        xT_done, hf_done, hi_done, lo_done = (Steps(sem(n + tag), 2) for n in ("xT_done", "hf_done", "hi_done", "lo_done"))
        with nc.Block() as block:
            @block.sync
            def _(sp):
                for steps in (xs_done, xT_done, hf_done, hi_done, lo_done):
                    steps.open(sp)
                for g in range(2):
                    if g:
                        sp.wait_ge(xT_done.sem, xT_done.done(KD - 1))
                    for t in range(4):
                        sp.dma_start(x[:, t], src[(g * 4 + t) * P:(g * 4 + t + 1) * P, :]).then_inc(x_in[t], 16)

            @block.scalar
            def _(act):
                with act.Fori(0, 2) as g:
                    act.wait_ge(xs_done.sem, xs_done.free(g))
                    for t in range(4):
                        act.wait_ge(x_in[t], g * 16 + 16)
                        act.activation(sq[:, :], x[:, t], ACT.Square, accum_out=ssq[:, t:t + 1]).then_inc(ssq_done, 1)
                        act.wait_ge(ssq_done, g * 4 + (t + 1))
                    act.activation(rstd[:, :], ssq[:, :], ACT.Sqrt, bias=K.eps[:, :], scale=1.0 / D).then_inc(root_done, 1)
                    for k in range(KD):
                        act.wait_ge(hf_done.sem, hf_done.done(g * KD + k))
                        act.activation(hhi[:, k, bass.ds(g * HALF, HALF)], hf[:, k % 2], ACT.Copy).then_inc(hi_done.sem, 1)

            @block.vector
            def _(dve):
                link = Chain(dve, sem("dve_norm" + tag))
                with dve.Fori(0, 2) as g:
                    link.enter(g, 5 + 2 * KD)
                    dve.wait_ge(root_done, g + 1)
                    link(dve.reciprocal(rstd[:, :], rstd[:, :]))
                    for t in range(4):
                        link(dve.tensor_scalar(x[:, t], x[:, t], rstd[:, t:t + 1], None, ALU.mult), *[xs_done.sem] * (t == 3))
                    for k in range(KD + 1):
                        if k < KD:
                            dve.wait_ge(xT_done.sem, xT_done.done(g * KD + k))
                            link(dve.tensor_scalar(hf[:, k % 2], pt[k % 2][:, :], a[:, k:k + 1], shift[:, k:k + 1],
                                                   ALU.mult, ALU.add), hf_done.sem)
                        if k:
                            dve.wait_ge(hi_done.sem, hi_done.done(g * KD + (k - 1)))
                            link(dve.tensor_tensor(hlo[:, k - 1, bass.ds(g * HALF, HALF)], hf[:, (k - 1) % 2],
                                                   hhi[:, k - 1, bass.ds(g * HALF, HALF)].bitcast(F32), ALU.subtract), lo_done.sem)
                link.leave(2)

            @block.tensor
            def _(pe):
                with pe.Fori(0, 2) as g:
                    pe.wait_ge(xs_done.sem, xs_done.done(g))
                    for k in range(KD):
                        pe.wait_ge(hf_done.sem, hf_done.free(g * KD + k))
                        for t in range(4):
                            last = pe.transpose(pt[k % 2][:, t * P:(t + 1) * P], x[:, t, k * P:(k + 1) * P], K.ident[:, :])
                        last.then_inc(xT_done.sem, 1)

def three_pass(pe, out, lhi, llo, rhi, rlo, k, n):
    pe.matmul(out, lhi, rhi, start=(k == 0), stop=False)
    pe.matmul(out, lhi, rlo, start=False, stop=False)
    return pe.matmul(out, llo, rhi, start=False, stop=(k == n - 1))

def token_gemm_phase(nc, tag, hhi, hlo, nk, wsrc, width, blocks, dst, keep):
    with ExitStack() as ctx:
        sem = ctx.enter_context(phase_semaphores(nc))
        sb = lambda n, s, d=F32: ctx.enter_context(nc.sbuf_tensor(n + tag, s, d))
        w = sb("gw", [P, 2, nk, width])
        whi = sb("gwhi", [P, 2, nk, width], F32R)
        wlo = sb("gwlo", [P, 2, nk, width], F32R)
        y = sb("gy", [P, 4, width])
        py = [ctx.enter_context(nc.psum_tensor(f"gpy{tag}{i}", [P, HALF], F32)) for i in range(4)]
        w_in = [one.start(blocks // 2) for one in keep.soft[0:2]]
        hi_done, lo_done = Steps(sem("whi_done" + tag), 2), Steps(sem("wlo_done" + tag), 2)
        y_mm, y_cp = Steps(sem("y_mm" + tag), 2 * TT), Steps(sem("y_cp" + tag), 4)
        y_out = [Steps(sem(f"y_out{tag}{i}"), 1, 16) for i in range(4)]
        with nc.Block() as block:
            @block.gpsimd
            def _(pool):
                for steps in (hi_done, lo_done, y_mm, y_cp, *y_out):
                    steps.open(pool)
                with pool.Fori(0, blocks // 2) as turn:
                    b = turn * 2
                    for s in range(2):
                        pool.wait_ge(lo_done.sem, lo_done.free(b + s))
                        pool.dma_start(w[:, s], wsrc[:, :, bass.ds((b + s) * width, width)]).then_inc(w_in[s].sem, 16)

            @block.scalar
            def _(act):
                def cut_high(b, s):
                    act.wait_ge(w_in[s].sem, w_in[s].value(b * 8 + 16))
                    act.wait_ge(y_mm.sem, y_mm.free((b + s) * TT + TT - 1))
                    act.activation(whi[:, s], w[:, s], ACT.Copy).then_inc(hi_done.sem, 1)

                with act.Fori(0, blocks // 2) as turn:
                    b = turn * 2
                    for s in range(2):
                        cut_high(b, s)

            @block.vector
            def _(dve):
                def cut_low(b, s):
                    dve.wait_ge(hi_done.sem, hi_done.done(b + s))
                    dve.tensor_tensor(wlo[:, s], w[:, s], whi[:, s].bitcast(F32), ALU.subtract).then_inc(lo_done.sem, 1)

                def copy_out(b, s):
                    for t in range(TT):
                        dve.wait_ge(y_mm.sem, y_mm.done((b + s) * TT + t))
                        dve.wait_ge(y_out[t % 4].sem, y_out[t % 4].free((b + s) * 2 + t // 4))
                        dve.tensor_copy(y[:, t % 4], py[t % 4][:, 0:width]).then_inc(y_cp.sem, 1)

                for s in range(2):
                    cut_low(0, s)
                if blocks > 2:
                    with dve.Fori(0, blocks // 2 - 1) as turn:
                        b = turn * 2
                        for s in range(2):
                            copy_out(b, s)
                            cut_low(b + 2, s)
                for s in range(2):
                    copy_out(blocks - 2, s)

            @block.sync
            def _(sp):
                with sp.Fori(0, blocks // 2) as turn:
                    b = turn * 2
                    for s in range(2):
                        for t in range(TT):
                            sp.wait_ge(y_cp.sem, y_cp.done((b + s) * TT + t))
                            sp.dma_start(dst[t * P:(t + 1) * P, bass.ds((b + s) * width, width)], y[:, t % 4]).then_inc(y_out[t % 4].sem, 16)
                for i in range(4):
                    sp.wait_ge(y_out[i].sem, y_out[i].done(2 * blocks - 1))

            @block.tensor
            def _(pe):
                with pe.Fori(0, blocks // 2) as turn:
                    b = turn * 2
                    for s in range(2):
                        pe.wait_ge(lo_done.sem, lo_done.done(b + s))
                        for t in range(TT):
                            pe.wait_ge(y_cp.sem, y_cp.free((b + s) * TT + t))
                            for k in range(nk):
                                last = three_pass(pe, py[t % 4][:, 0:width], hhi[:, k, t * P:(t + 1) * P], hlo[:, k, t * P:(t + 1) * P],
                                                  whi[:, s, k], wlo[:, s, k], k, nk)
                            last.then_inc(y_mm.sem, 1)

def place(head):
    return (head % 2) * 4 + head // 2

LEVELS = [64, 32, 16, 8, 4, 2, 1]
PER_ACT, PER_DVE, PER_POOL = 39, 60, 6
SWT_LEVEL = 3

def mixer_phase(nc, proj, yhi, ylo, keep):
    K = keep
    W = COL_GL
    with ExitStack() as ctx:
        sem = ctx.enter_context(phase_semaphores(nc))
        sb = lambda n, s, d=F32: ctx.enter_context(nc.sbuf_tensor(n, s, d))
        prj = sb("prj", [P, 2, W])
        masks = sb("masks", [P, len(LEVELS) + 1, P], I32)
        mt = sb("mt", [P, 3, P], I32)
        ti, si = sb("ti", [P, P], I32), sb("si", [P, P], I32)
        reset = sb("reset", [P, NH * P])
        lb, omlb = sb("lb", [P, NH]), sb("omlb", [P, NH])
        qT, kT, fT, lf, b = (sb(n, [P, NH, P]) for n in ("hqT", "hkT", "hfT", "hlf", "hb"))
        dif, ex, wl = sb("dif", [P, 2, NH * P]), sb("ex", [P, 2, NH * P]), sb("wl", [P, 2, NH, P])
        S = sb("hS", [P, NH, P])
        E0, qd, kd, kdt, dl = (sb(n, [P, NH, P]) for n in ("hE0", "hqd", "hkd", "hkdt", "hdl"))
        state = sb("state", [P, NH, P])
        o, osq, sg = sb("ho", [P, NH, P]), sb("hosq", [P, NH * P]), sb("hsg", [P, NH * P])
        oss = sb("hoss", [P, NH])
        y2 = sb("y2", [P, 2, 512])
        sqb, ss10 = sb("sqb", [P, 640]), sb("ss10", [P, 10])
        qkn = sb("qkn", [P, 10, HD])
        kk = sb("kk", [P, SWKV, 2, HD])
        qT2 = sb("qT2", [P, 4, P])
        kTs = sb("kTs", [P, 2, SWKV, P])
        vr = sb("vr", [P, 2, P])
        pm = sb("pm", [HD, HD])
        sc = sb("sc", [P, SWH, 193])
        pb = sb("pb", [P, SWH, 257])
        mx, den = sb("smx", [P, SWH]), sb("sden", [P, SWH])
        pTc, pTp = sb("pTc", [P, SWH, P]), sb("pTp", [P, SWH, P])
        yf = sb("yf", [P, 8, P])
        gate = sb("hgate", [P, 512])
        bk = [ctx.enter_context(nc.psum_tensor(f"mbk{i}", [P, HALF], F32)) for i in range(4)]
        big = ctx.enter_context(nc.psum_tensor("mbig", [P, SWH, 256], F32))

        prj_in = [sem(f"prj_in{i}") for i in range(2)]
        names = ("tile_done", "hgT_mm", "q_cp", "sig_done", "f_done", "log_done", "e0_done", "kd_ready", "kdT_mm", "kdT_cp",
                 "s_done", "qd_done", "o_mm", "su_mm", "osq_done", "ssig_done", "oroot", "oss_done", "sq_done", "ss_done", "qkroot",
                 "qk_ready", "swT_mm", "kT2_cp", "inv_done", "gate_ready", "sc_mm", "sc_low", "sc_all", "negmax", "exp_done", "pT_mm", "pTc_cp",
                 "pTp_cp", "osw_mm", "y_done", "yT_mm", "yhi_done", "blast_dif", "blast_ex", "gsg_done", "prep", "den_done")
        s = {n: sem("m_" + n) for n in names}
        tile_free = Steps(sem("tile_free"), 2)
        dif_done, ex_done, wl_done = sem("dif_done"), sem("ex_done"), sem("wl_done")
        lev_mm = Steps(sem("lev_mm"), 2)
        lev_used = Steps(sem("lev_used"), 2)
        state_up, yf_done = Steps(sem("state_up"), 1), Steps(sem("yf_done"), 1)
        NL = len(LEVELS)
        settled = sem("m_settled")
        with nc.Block() as block:
            @block.sync
            def _(sp):
                for steps in (tile_free, lev_mm, lev_used, state_up, yf_done):
                    steps.open(sp)
                with sp.Fori(0, TT // 2) as turn:
                    for p in range(2):
                        sp.wait_ge(tile_free.sem, tile_free.free(turn * 2 + p))
                        sp.dma_start(prj[:, p], proj[bass.ds((turn * 2 + p) * P, P), 0:W]).then_inc(prj_in[p], 16)

            @block.gpsimd
            def _(pool):
                link = Chain(pool, sem("pool_mix"))
                link(pool.iota(ti[:, :], pattern=[[1, P]], base=0, channel_multiplier=0))
                link(pool.iota(si[:, :], pattern=[[0, P]], base=0, channel_multiplier=1))
                link(pool.memset(state[:, :, :], 0.0))
                link(pool.memset(kTs[:, :, :, :], 0.0))
                link(pool.memset(vr[:, :, :], 0.0))
                link(pool.memset(pm[:, :], NEG))
                link(pool.memset(pb[:, :, :], 0.0))
                link(pool.memset(sc[:, :, :], NEG))
                link(pool.memset(reset[:, :], 1.0))
                link(pool.memset(reset[:, :].rearrange("p (h t) -> p h t", h=NH)[:, :, 0:1], 0.0))
                link(pool.memset(S[:, :, :], 0.0))
                link(pool.tensor_copy(sc[:, :, 192:193].rearrange("p (c j) one -> p j c one", c=2),
                                      K.sink[:, :, None].rearrange("p (j c) one -> p j c one", c=2)), s["prep"])
                with pool.Fori(0, TT // 2) as turn:
                    link.enter(turn, 2 * PER_POOL)
                    for p in range(2):
                        n = turn * 2 + p + 1
                        pool.wait_ge(s["inv_done"], n)
                        link(pool.tensor_tensor(qkn[:, :, :], prj[:, p, COL_SQ:COL_SQ + 640].rearrange("p (a d) -> p a d", d=HD),
                                                ss10[:, :, None].to_broadcast([P, 10, HD]), ALU.mult))
                        link.together([pool.tensor_tensor(kk[:, :, 0], qkn[:, 8:10], K.kw[:, None, :].to_broadcast([P, 2, HD]), ALU.mult),
                                       pool.tensor_tensor(kk[:, :, 1], qkn[:, 8:10], K.kw[:, None, :].to_broadcast([P, 2, HD]), ALU.mult),
                                       pool.tensor_tensor(qkn[:, 0:8], qkn[:, 0:8], K.qw[:, None, :].to_broadcast([P, 8, HD]), ALU.mult)],
                                      s["qk_ready"])
                        pool.wait_ge(s["gsg_done"], n)
                        link(pool.tensor_tensor(gate[:, :], prj[:, p, COL_HG:COL_HG + 512], sg[:, :], ALU.mult))
                        gv = gate[:, :].rearrange("p (h d) -> p h d", h=NH)
                        link(pool.tensor_tensor(gv, gv, K.hgw[:, None, :].to_broadcast([P, NH, P]), ALU.mult), s["gate_ready"])
                link.leave(TT // 2)

            @block.scalar
            def _(act):
                link = Chain(act, sem("act_mix"))
                act.wait_ge(s["prep"], 2)
                with act.Fori(0, TT // 2) as turn:
                    link.enter(turn, 2 * PER_ACT)
                    for p in range(2):
                        t = turn * 2 + p
                        n = t + 1
                        act.wait_ge(s["hgT_mm"], n)
                        link(act.activation(fT[:, :, :], bk[1][:, :].rearrange("p (h t) -> p h t", h=NH), ACT.Sigmoid), s["sig_done"])
                        link(act.activation(sqb[:, :], prj[:, p, COL_SQ:COL_SQ + 640], ACT.Square), s["sq_done"])
                        link.together([act.activation(sg[:, :], prj[:, p, COL_HG:COL_HG + 512], ACT.Sigmoid),
                                       act.activation(vr[:, p], prj[:, p, COL_SV:COL_SV + P], ACT.Copy)], s["gsg_done"])
                        act.wait_ge(s["f_done"], n)
                        link(act.activation(lf[:, :, :], fT[:, :, :], ACT.Ln), s["log_done"])
                        act.wait_ge(s["ss_done"], n)
                        link(act.activation(ss10[:, :], ss10[:, :], ACT.Sqrt, bias=K.eps[:, :], scale=1.0 / HD), s["qkroot"])
                        for l, m in enumerate(LEVELS):
                            act.wait_ge(dif_done, t * NL + (l + 1))
                            dv = dif[:, l % 2].rearrange("p (n w) -> p n w", w=2 * m)
                            ev = ex[:, l % 2].rearrange("p (n w) -> p n w", w=2 * m)
                            link.together([act.activation(ev[:, :, 0:m], dv[:, :, 0:m], ACT.Exp, scale=-1.0),
                                           act.activation(ev[:, :, m:], dv[:, :, m:], ACT.Exp)], ex_done)
                            if l == SWT_LEVEL + 1:
                                act.wait_ge(s["swT_mm"], n)
                                link.together([act.activation(qT2[:, :, :], big[:, 0:2].rearrange("p a (b t) -> p (a b) t", b=2), ACT.Copy),
                                               act.activation(kTs[:, p], big[:, 2].rearrange("p (g t) -> p g t", g=SWKV), ACT.Copy)], s["kT2_cp"])
                        link(act.activation(E0[:, :, :], b[:, :, :], ACT.Exp), s["e0_done"])
                        act.wait_ge(s["blast_dif"], n)
                        link(act.activation(kd[:, :, :], dl[:, :, :], ACT.Exp, scale=-1.0), s["blast_ex"])
                        act.wait_ge(s["sc_mm"], n)
                        link(act.activation(sc[HD:P, :, HD:192], big[HD:P, :, HD:192], ACT.Copy, scale=HD ** -0.5), s["sc_low"])
                        act.wait_ge(s["kdT_mm"], n)
                        link(act.activation(kdt[:, :, :], bk[1][:, :].rearrange("p (h t) -> p h t", h=NH), ACT.Copy), s["kdT_cp"])
                        act.wait_ge(s["o_mm"], n)
                        link(act.activation(o[:, :, :], bk[0][:, :].rearrange("p (h t) -> p h t", h=NH), ACT.Copy))
                        link(act.activation(osq[:, :], o[:, :, :].rearrange("p h t -> p (h t)"), ACT.Square), s["osq_done"])
                        act.wait_ge(s["negmax"], n)
                        link.together([act.activation(pb[:, h, 64:257], sc[:, h, :], ACT.Exp, bias=mx[:, h:h + 1], accum_out=den[:, h:h + 1])
                                       for h in range(SWH)], s["exp_done"])
                        act.wait_ge(s["oss_done"], n)
                        link(act.activation(oss[:, :], oss[:, :], ACT.Sqrt, bias=K.eps[:, :], scale=1.0 / P), s["oroot"])
                        act.wait_ge(s["pT_mm"], n)
                        link(act.activation(pTc[:, :, :], big[:, 0:4].rearrange("p a (b t) -> p (a b) t", b=2), ACT.Copy), s["pTc_cp"])
                        act.wait_ge(yf_done.sem, yf_done.done(t))
                        link(act.activation(yhi[:, :, bass.ds(t * P, P)], yf[:, :, :], ACT.Copy), s["yhi_done"])
                link.leave(TT // 2)

            @block.vector
            def _(dve):
                link = Chain(dve, sem("dve_mix"))
                dve.wait_ge(s["prep"], 1)
                link(dve.memset(mt[:, 0], 0))
                for l, m in enumerate(LEVELS):
                    sh = m.bit_length() - 1
                    link(dve.tensor_single_scalar(mt[:, 0], ti[:, :], sh, ALU.logical_shift_right))
                    link(dve.tensor_single_scalar(mt[:, 1], si[:, :], sh, ALU.logical_shift_right))
                    link(dve.tensor_single_scalar(mt[:, 2], mt[:, 0], 1, ALU.bitwise_and))
                    link(dve.tensor_tensor(mt[:, 0], mt[:, 0], mt[:, 1], ALU.subtract))
                    link(dve.tensor_single_scalar(mt[:, 0], mt[:, 0], 1.0, ALU.is_equal))
                    link(dve.tensor_tensor(masks[:, l], mt[:, 0], mt[:, 2], ALU.mult))
                link(dve.tensor_tensor(masks[:, NL], ti[:, :], si[:, :], ALU.is_equal))
                link(dve.tensor_copy(lb[:, :], K.lbs[:, :]))
                link(dve.tensor_scalar(omlb[:, :], lb[:, :], -1.0, 1.0, ALU.mult, ALU.add), s["prep"])
                with dve.Fori(0, TT // 2) as turn:
                    link.enter(turn, 2 * PER_DVE)
                    for p in range(2):
                        t = turn * 2 + p
                        n = t + 1
                        dve.wait_ge(s["hgT_mm"], n)
                        link(dve.tensor_copy(qT[:, :, :], bk[0][:, :].rearrange("p (h t) -> p h t", h=NH)), s["q_cp"])
                        dve.wait_ge(s["sig_done"], n)
                        link.together([dve.tensor_scalar(fT[:, h], fT[:, h], omlb[:, h:h + 1], lb[:, h:h + 1], ALU.mult, ALU.add)
                                       for h in range(NH)], s["f_done"])
                        link(dve.tensor_scalar(kT[:, :, :], fT[:, :, :], -1.0, 1.0, ALU.mult, ALU.add))
                        dve.wait_ge(s["sq_done"], n)
                        link(dve.tensor_reduce(ss10[:, :], sqb[:, :].rearrange("p (a d) -> p a d", d=HD), AX, ALU.add), s["ss_done"])
                        dve.wait_ge(s["log_done"], n)
                        bf = b[:, :, :].rearrange("p h t -> p (h t)")
                        qf, kf = (x[:, :, :].rearrange("p h t -> p (h t)") for x in (qT, kT))
                        link(dve.tensor_tensor_scan(bf, reset[:, :], lf[:, :, :].rearrange("p h t -> p (h t)"), 0.0, ALU.mult, ALU.add))

                        def level_dif(l):
                            m = LEVELS[l]
                            bv = bf.rearrange("p (n w) -> p n w", w=2 * m)
                            link(dve.tensor_tensor(dif[:, l % 2].rearrange("p (n w) -> p n w", w=2 * m), bv,
                                                   bv[:, :, m - 1:m].to_broadcast([P, NH * P // (2 * m), 2 * m]), ALU.subtract), dif_done)

                        def level_take(l):
                            dve.wait_ge(lev_mm.sem, lev_mm.done(t * (NL + 1) + l))
                            settle(dve, settled)
                            link(dve.copy_predicated(S[:, :, :], masks[:, l:l + 1, :].to_broadcast([P, NH, P]),
                                                     bk[2 + l % 2][:, :].rearrange("p (h t) -> p h t", h=NH)), lev_used.sem)

                        level_dif(0)
                        for l, m in enumerate(LEVELS):
                            if l + 1 < NL:
                                level_dif(l + 1)
                            dve.wait_ge(ex_done, t * NL + (l + 1))
                            dve.wait_ge(lev_mm.sem, lev_mm.free(t * (NL + 1) + l))
                            w = wl[:, l % 2].rearrange("p h t -> p (h t)").rearrange("p (n w) -> p n w", w=2 * m)
                            ev = ex[:, l % 2].rearrange("p (n w) -> p n w", w=2 * m)
                            kv, qv = (x.rearrange("p (n w) -> p n w", w=2 * m) for x in (kf, qf))
                            link.together([dve.tensor_tensor(w[:, :, 0:m], kv[:, :, 0:m], ev[:, :, 0:m], ALU.mult),
                                           dve.tensor_tensor(w[:, :, m:], qv[:, :, m:], ev[:, :, m:], ALU.mult)], wl_done)
                            if l == 0:
                                dve.wait_ge(s["qkroot"], n)
                                link(dve.reciprocal(ss10[:, :], ss10[:, :]), s["inv_done"])
                            else:
                                level_take(l - 1)
                        link(dve.tensor_tensor(dl[:, :, :], b[:, :, :], b[:, :, P - 1:P].to_broadcast([P, NH, P]), ALU.subtract), s["blast_dif"])
                        dve.wait_ge(s["e0_done"], n)
                        link(dve.tensor_tensor(qd[:, :, :], qT[:, :, :], E0[:, :, :], ALU.mult), s["qd_done"])
                        dve.wait_ge(s["blast_ex"], n)
                        link(dve.tensor_tensor(kd[:, :, :], kd[:, :, :], kT[:, :, :], ALU.mult), s["kd_ready"])
                        level_take(NL - 1)
                        level_take(NL)
                        dve.sem_inc(s["s_done"], 1)
                        dve.wait_ge(s["sc_mm"], n)
                        link.together([dve.scalar_tensor_tensor(sc[0:HD, :, 0:HD], big[0:HD, :, 0:HD], HD ** -0.5,
                                                                pm[:, None, :].to_broadcast([HD, SWH, HD]), ALU.mult, ALU.add),
                                       dve.tensor_scalar(sc[0:HD, :, HD:P], big[0:HD, :, HD:P], HD ** -0.5, None, ALU.mult)])
                        link(dve.memset(pm[:, :], 0.0))
                        dve.wait_ge(s["sc_low"], n)
                        link(dve.tensor_reduce(mx[:, :], sc[:, :, :], AX, ALU.max))
                        link(dve.tensor_scalar(mx[:, :], mx[:, :], -1.0, None, ALU.mult), s["negmax"])
                        dve.wait_ge(s["su_mm"], n)
                        link.together([dve.scalar_tensor_tensor(state[:, h], state[:, h], E0[:, h, P - 1:P], bk[1][:, h * P:(h + 1) * P],
                                                                ALU.mult, ALU.add) for h in range(NH)], state_up.sem)
                        dve.wait_ge(s["osq_done"], n)
                        link(dve.tensor_reduce(oss[:, :], osq[:, :].rearrange("p (a d) -> p a d", d=P), AX, ALU.add), s["oss_done"])
                        dve.wait_ge(s["pT_mm"], n)
                        link(dve.tensor_copy(pTp[:, :, :], big[:, 4:8].rearrange("p a (b t) -> p (a b) t", b=2)), s["pTp_cp"])
                        dve.wait_ge(s["exp_done"], n)
                        link(dve.reciprocal(den[:, :], den[:, :]))
                        dve.wait_ge(s["oroot"], n)
                        link(dve.reciprocal(oss[:, :], oss[:, :]))
                        dve.wait_ge(s["gate_ready"], n)
                        yv = y2[:, 0].rearrange("p (h d) -> p h d", h=NH)
                        link(dve.tensor_tensor(yv, o[:, :, :], oss[:, :, None].to_broadcast([P, NH, P]), ALU.mult))
                        link(dve.tensor_tensor(y2[:, 0], y2[:, 0], gate[:, :], ALU.mult))
                        dve.wait_ge(s["osw_mm"], n)
                        link(dve.tensor_tensor(y2[:, 1].rearrange("p (j c d) -> p j c d", c=2, d=HD),
                                               bk[2][:, :].rearrange("p (j c d) -> p j c d", c=2, d=HD),
                                               den[:, :, None].rearrange("p (c j) one -> p j c one", c=2).to_broadcast([P, 4, 2, HD]),
                                               ALU.mult), s["y_done"], tile_free.sem)
                        dve.wait_ge(s["yT_mm"], n)
                        for c in range(2):
                            link(dve.tensor_copy(yf[:, 4 * c:4 * c + 4], bk[3 * c][:, :].rearrange("p (a t) -> p a t", a=4)),
                                 *[yf_done.sem] * c)
                        dve.wait_ge(s["yhi_done"], n)
                        link(dve.tensor_tensor(ylo[:, :, bass.ds(t * P, P)], yf[:, :, :], yhi[:, :, bass.ds(t * P, P)].bitcast(F32), ALU.subtract))
                link.leave(TT // 2)

            @block.tensor
            def _(pe):
                with pe.Fori(0, TT // 2) as turn:
                    for p in range(2):
                        t = turn * 2 + p
                        n = t + 1
                        pe.wait_ge(prj_in[p], turn * 16 + 16)
                        pe.wait_ge(state_up.sem, state_up.free(t))
                        pe.wait_ge(yf_done.sem, yf_done.free(t))
                        for c in range(2):
                            for h in range(NH):
                                last = pe.transpose(bk[c][:, h * P:(h + 1) * P], prj[:, p, c * 512 + h * P:c * 512 + (h + 1) * P], K.ident[:, :])
                        last.then_inc(s["hgT_mm"], 1)
                        for l in range(NL + 1):
                            if l < NL:
                                pe.wait_ge(wl_done, t * NL + (l + 1))
                            pe.wait_ge(lev_used.sem, lev_used.free(t * (NL + 1) + l))
                            for h in range(NH):
                                lhs, rhs = (wl[:, l % 2, h], wl[:, l % 2, h]) if l < NL else (kT[:, h], qT[:, h])
                                last = pe.matmul(bk[2 + l % 2][:, h * P:(h + 1) * P], lhs, rhs, start=True, stop=True)
                            last.then_inc(lev_mm.sem, 1)
                            if l == SWT_LEVEL:
                                pe.wait_ge(s["qk_ready"], n)
                                for a in range(4):
                                    pe.transpose(big[:, a // 2, (a % 2) * P:(a % 2 + 1) * P], qkn[:, 2 * a:2 * a + 2].rearrange("p a d -> p (a d)"), K.ident[:, :])
                                for g in range(SWKV):
                                    last = pe.transpose(big[:, 2, g * P:(g + 1) * P], kk[:, g].rearrange("p a d -> p (a d)"), K.ident[:, :])
                                last.then_inc(s["swT_mm"], 1)
                            if l == SWT_LEVEL + 2:
                                pe.wait_ge(s["kT2_cp"], n)
                                for h in range(SWH):
                                    r = (h % 2) * HD
                                    q = qT2[r:r + HD, h // 2]
                                    pe.matmul(big[:, place(h), 0:HD], q, kTs[r:r + HD, 1 - p, h // 4, HD:P], start=True, stop=True)
                                    last = pe.matmul(big[:, place(h), HD:192], q, kTs[r:r + HD, p, h // 4], start=True, stop=True)
                                last.then_inc(s["sc_mm"], 1)
                        pe.wait_ge(s["kd_ready"], n)
                        for h in range(NH):
                            last = pe.transpose(bk[1][:, h * P:(h + 1) * P], kd[:, h], K.ident[:, :])
                        last.then_inc(s["kdT_mm"], 1)
                        pe.wait_ge(s["s_done"], n)
                        pe.wait_ge(s["qd_done"], n)
                        for h in range(NH):
                            v = prj[:, p, COL_HI + h * P:COL_HI + (h + 1) * P]
                            pe.matmul(bk[0][:, h * P:(h + 1) * P], S[:, h], v, start=True, stop=False)
                            last = pe.matmul(bk[0][:, h * P:(h + 1) * P], qd[:, h], state[:, h], start=False, stop=True)
                        last.then_inc(s["o_mm"], 1)
                        pe.wait_ge(s["kdT_cp"], n)
                        for h in range(NH):
                            last = pe.matmul(bk[1][:, h * P:(h + 1) * P], kdt[:, h], prj[:, p, COL_HI + h * P:COL_HI + (h + 1) * P],
                                             start=True, stop=True)
                        last.then_inc(s["su_mm"], 1)
                        pe.wait_ge(s["exp_done"], n)
                        for h in range(SWH):
                            pe.transpose(big[:, h // 2, (h % 2) * P:(h % 2 + 1) * P], pb[:, h, P:256], K.ident[:, :])
                            last = pe.transpose(big[:, 4 + h // 2, (h % 2) * P:(h % 2 + 1) * P], pb[:, h, 0:P], K.ident[:, :])
                        last.then_inc(s["pT_mm"], 1)
                        pe.wait_ge(s["pTc_cp"], n)
                        pe.wait_ge(s["pTp_cp"], n)
                        for h in range(SWH):
                            g = (h // 4) * HD
                            pe.matmul(bk[2][:, h * HD:(h + 1) * HD], pTc[:, place(h)], vr[:, p, g:g + HD], start=True, stop=False)
                            last = pe.matmul(bk[2][:, h * HD:(h + 1) * HD], pTp[:, place(h)], vr[:, 1 - p, g:g + HD], start=False, stop=True)
                        last.then_inc(s["osw_mm"], 1)
                        pe.wait_ge(s["y_done"], n)
                        for c in range(2):
                            for a in range(4):
                                last = pe.transpose(bk[3 * c][:, a * P:(a + 1) * P], y2[:, c, a * P:(a + 1) * P], K.ident[:, :])
                        last.then_inc(s["yT_mm"], 1)

def merge_phase(nc, yhi, ylo, proj, w_branch, w_out, x, gate1_dram, x1, keep):
    K = keep
    NS = 2 * D // HALF
    with ExitStack() as ctx:
        sem = ctx.enter_context(phase_semaphores(nc))
        sb = lambda n, s, d=F32: ctx.enter_context(nc.sbuf_tensor(n, s, d))
        wr = sb("mwr", [P, 2, 4, HALF])
        whi, wlo = sb("mwhi", [P, 2, 4, HALF], F32R), sb("mwlo", [P, 2, 4, HALF], F32R)
        gl = sb("mgl", [P, 2, HALF])
        gs = sb("mgs", [P, 2, HALF])
        pr = sb("mpr", [P, 2, HALF])
        z = sb("mz", [P, TT, D])
        acc = [ctx.enter_context(nc.psum_tensor(f"mp{i}", [P, HALF], F32)) for i in range(4)]
        w_in = [sem(f"mw_in{i}") for i in range(2)]
        hi_done, lo_done = sem("mhi_done"), sem("mlo_done")
        gl_in = [one.start(2 * TT) for one in keep.soft[0:2]]
        z_mm, z_prod, gsig = sem("z_mm"), sem("z_prod"), sem("gsig")
        PASS = [(h, n) for h in range(2) for n in range(2)]
        with nc.Block() as block:
            @block.sync
            def _(sp):
                for i, (h, n) in enumerate(PASS):
                    if i >= 2:
                        sp.wait_ge(lo_done, i - 1)
                    sp.dma_start(wr[:, i % 2], w_branch[0, n].rearrange("(k p) d -> p k d", p=P)[:, :, h * HALF:(h + 1) * HALF]).then_inc(w_in[i % 2], 16)

            @block.gpsimd
            def _(pool):
                for i, (h, n) in enumerate(PASS):
                    for t in range(TT):
                        u = i * TT + t
                        if u >= 2:
                            pool.wait_ge(gsig, u - 1)
                        c = COL_GL + n * D + h * HALF
                        pool.dma_start(gl[:, u % 2], proj[t * P:(t + 1) * P, c:c + HALF]).then_inc(gl_in[u % 2].sem, 16)

            @block.scalar
            def _(act):
                def cut_high(i):
                    act.wait_ge(w_in[i % 2], 16 * (i // 2 + 1))
                    if i >= 2:
                        act.wait_ge(z_mm, (i - 1) * TT)
                    act.activation(whi[:, i % 2], wr[:, i % 2], ACT.Copy).then_inc(hi_done, 1)

                cut_high(0)
                cut_high(1)
                for i in range(4):
                    for t in range(TT):
                        u = i * TT + t
                        act.wait_ge(gl_in[u % 2].sem, gl_in[u % 2].value(16 * (u // 2 + 1)))
                        if u >= 2:
                            act.wait_ge(z_prod, u - 1)
                            act.wait_ge(gsig, u - 1)
                        act.activation(gs[:, u % 2], gl[:, u % 2], ACT.Sigmoid).then_inc(gsig, 1)
                    if i + 2 < 4:
                        cut_high(i + 2)

            @block.vector
            def _(dve):
                link = Chain(dve, sem("dve_merge"))

                def cut_low(i):
                    dve.wait_ge(hi_done, i + 1)
                    link(dve.tensor_tensor(wlo[:, i % 2], wr[:, i % 2], whi[:, i % 2].bitcast(F32), ALU.subtract), lo_done)

                cut_low(0)
                cut_low(1)
                for i, (h, n) in enumerate(PASS):
                    for t in range(TT):
                        u = i * TT + t
                        zt = z[:, t, h * HALF:(h + 1) * HALF]
                        dve.wait_ge(z_mm, u + 1)
                        dve.wait_ge(gsig, u + 1)
                        link(dve.tensor_tensor(pr[:, u % 2] if n else zt, acc[u % 4][:, :], gs[:, u % 2], ALU.mult), z_prod)
                        if n:
                            link(dve.tensor_tensor(zt, zt, pr[:, u % 2], ALU.add))
                    if i + 2 < 4:
                        cut_low(i + 2)

            @block.tensor
            def _(pe):
                for i, (h, n) in enumerate(PASS):
                    pe.wait_ge(lo_done, i + 1)
                    for t in range(TT):
                        u = i * TT + t
                        if u >= 4:
                            pe.wait_ge(z_prod, u - 3)
                        for k in range(4):
                            last = three_pass(pe, acc[u % 4][:, :], yhi[:, 4 * n + k, t * P:(t + 1) * P], ylo[:, 4 * n + k, t * P:(t + 1) * P],
                                              whi[:, i % 2, k], wlo[:, i % 2, k], k, 4)
                        last.then_inc(z_mm, 1)

        wo = wr
        pt = acc[0:2]
        zt_mm, zf_done, zhi_done = Steps(sem("zt_mm"), 2), Steps(sem("zf_done"), 2), Steps(sem("zhi_done"), 2)
        zlo_done = sem("zlo_done")
        wo_in, wohi, wolo = sem("wo_in"), sem("wohi"), sem("wolo")
        xt = sb("mxt", [P, 2, HALF])
        gate1, gate1_in = sb("gate1", [P, D]), sem("gate1_in")
        xt_in = [one.start(TT) for one in keep.soft[2:4]]
        m_read = sem("m_read")
        m_mm, m_done, x1_out = sem("m_mm"), sem("m_done"), [sem(f"x1_out{i}") for i in range(2)]
        with nc.Block() as block:
            units = [(j, t) for j in range(2) for t in range(TT)]

            @block.sync
            def _(sp):
                sp.dma_start(gate1[:, :], gate1_dram.to_broadcast([P, D])).then_inc(gate1_in, 16)
                for j in range(2):
                    if j:
                        sp.wait_ge(wolo, 2)
                    for q in range(2):
                        sp.dma_start(wo[:, q], w_out[0].rearrange("(k p) d -> p k d", p=P)[:, 4 * q:4 * q + 4, j * HALF:(j + 1) * HALF]).then_inc(wo_in, 16)
                for u, (j, t) in enumerate(units):
                    sp.wait_ge(m_done, u + 1)
                    sp.dma_start(x1[t * P:(t + 1) * P, j * HALF:(j + 1) * HALF], xt[:, u % 2]).then_inc(x1_out[u % 2], 16)
                for i in range(2):
                    sp.wait_ge(x1_out[i], 16 * TT)

            @block.gpsimd
            def _(pool):
                for u, (j, t) in enumerate(units):
                    if u >= 2:
                        pool.wait_ge(x1_out[u % 2], 16 * (u // 2))
                    pool.dma_start(xt[:, u % 2], x[t * P:(t + 1) * P, j * HALF:(j + 1) * HALF]).then_inc(xt_in[u % 2].sem, 16)

            @block.scalar
            def _(act):
                def cut_high(j):
                    act.wait_ge(wo_in, 32 * (j + 1))
                    if j:
                        act.wait_ge(m_mm, TT)
                        act.wait_ge(wohi, 2)
                    for q in range(2):
                        act.activation(whi[:, q], wo[:, q], ACT.Copy).then_inc(wohi, 1)

                for u in range(2 * KD):
                    act.wait_ge(zf_done.sem, u + 3)
                    act.activation(yhi[:, u % KD, (u // KD) * HALF:(u // KD + 1) * HALF], gs[:, u % 2], ACT.Copy).then_inc(zhi_done.sem, 1)
                cut_high(0)
                cut_high(1)

            @block.vector
            def _(dve):
                link = Chain(dve, sem("dve_out"))
                for steps in (zt_mm, zf_done, zhi_done):
                    steps.open(dve)
                for u in range(2 * KD):
                    dve.wait_ge(zt_mm.sem, zt_mm.done(u))
                    link(dve.tensor_copy(gs[:, u % 2], pt[u % 2][:, :]), zf_done.sem)
                    dve.wait_ge(zhi_done.sem, zhi_done.done(u))
                    dst = (slice(None), u % KD, slice((u // KD) * HALF, (u // KD + 1) * HALF))
                    link(dve.tensor_tensor(ylo[dst], gs[:, u % 2], yhi[dst].bitcast(F32), ALU.subtract), zlo_done)
                dve.wait_ge(gate1_in, 16)
                for j in range(2):
                    dve.wait_ge(wohi, 2 * (j + 1))
                    for q in range(2):
                        link(dve.tensor_tensor(wlo[:, q], wo[:, q], whi[:, q].bitcast(F32), ALU.subtract), wolo)
                    for t in range(TT):
                        u = j * TT + t
                        dve.wait_ge(m_mm, u + 1)
                        dve.wait_ge(xt_in[u % 2].sem, xt_in[u % 2].value(16 * (u // 2 + 1)))
                        link(dve.tensor_tensor(pr[:, u % 2], acc[u % 4][:, :], gate1[:, j * HALF:(j + 1) * HALF], ALU.mult), m_read)
                        link(dve.tensor_tensor(xt[:, u % 2], xt[:, u % 2], pr[:, u % 2], ALU.add), m_done)

            @block.tensor
            def _(pe):
                for u in range(2 * KD):
                    k, g = u % KD, u // KD
                    pe.wait_ge(zf_done.sem, zf_done.free(u))
                    for t in range(4):
                        last = pe.transpose(pt[u % 2][:, t * P:(t + 1) * P], z[:, 4 * g + t, k * P:(k + 1) * P], K.ident[:, :])
                    last.then_inc(zt_mm.sem, 1)
                pe.wait_ge(zlo_done, 2 * KD)
                for u, (j, t) in enumerate(units):
                    pe.wait_ge(wolo, 2 * (j + 1))
                    if u >= 4:
                        pe.wait_ge(m_read, u - 3)
                    for k in range(KD):
                        last = three_pass(pe, acc[u % 4][:, :], yhi[:, k, t * P:(t + 1) * P], ylo[:, k, t * P:(t + 1) * P],
                                          whi[:, k // 4, k % 4], wlo[:, k // 4, k % 4], k, KD)
                    last.then_inc(m_mm, 1)

HC = 2 * HEADS
NBEST = TOPK * TOPK

def route_phase(nc, h2hi, h2lo, w_query, sub_keys, TV, TI, keep):
    K = keep
    with ExitStack() as ctx:
        sem = ctx.enter_context(phase_semaphores(nc))
        sb = lambda n, s, d=F32: ctx.enter_context(nc.sbuf_tensor(n, s, d))
        w = sb("qw_raw", [P, 2, KD, P])
        whi, wlo = sb("qwhi", [P, 2, KD, P], F32R), sb("qwlo", [P, 2, KD, P], F32R)
        kraw, kT = sb("kraw", [P, 2, P]), sb("keysT", [P, 2, P])
        qT = sb("rqT", [P, 2, T])
        s = sb("rs", [P, 2, TT, NKEYS])
        s2 = sb("rs2", [P, TT, NKEYS])
        tv, tix, tf = sb("rtv", [P, TT, TOPK]), sb("rti", [P, TT, TOPK], U32), sb("rtf", [P, TT, TOPK])
        pq = [ctx.enter_context(nc.psum_tensor(f"rpq{i}", [P, HALF], F32)) for i in range(2)]
        pk = ctx.enter_context(nc.psum_tensor("rpk", [P, P], F32))
        psc = [ctx.enter_context(nc.psum_tensor(f"rps{i}", [P, 4, NKEYS], F32)) for i in range(2)]
        w_in, k_in = [sem(f"rw_in{i}") for i in range(2)], [sem(f"rk_in{i}") for i in range(2)]
        hi_done, lo_done = Steps(sem("rhi_done"), 2), Steps(sem("rlo_done"), 2)
        q_mm, q_cp = Steps(sem("rq_mm"), 2), Steps(sem("rq_cp"), 2)
        k_mm, k_cp = Steps(sem("rk_mm"), 2), Steps(sem("rk_cp"), 1)
        s_mm, s_cp = Steps(sem("rs_mm"), 2), Steps(sem("rs_cp"), 2)
        top_done = Steps(sem("rtop_done"), 2)
        settled = sem("r_settled")
        wv = w_query.rearrange("(k p) n -> p k n", p=P)
        kv = sub_keys.rearrange("h c k d -> (h c) k d")
        with nc.Block() as block:
            @block.sync
            def _(sp):
                for steps in (hi_done, lo_done, q_mm, q_cp, k_mm, k_cp, s_mm, s_cp, top_done):
                    steps.open(sp)
                with sp.Fori(0, HC // 2) as turn:
                    for p in range(2):
                        c = turn * 2 + p
                        sp.wait_ge(lo_done.sem, lo_done.free(c))
                        sp.dma_start(w[:, p], wv[:, :, bass.ds(c * P, P)]).then_inc(w_in[p], 16)
                        sp.wait_ge(k_mm.sem, k_mm.free(c))
                        sp.dma_start(kraw[:, p], kv[bass.ds(c, 1)].rearrange("o k d -> (o k) d")).then_inc(k_in[p], 16)

            @block.scalar
            def _(act):
                with act.Fori(0, HC // 2) as turn:
                    for p in range(2):
                        c = turn * 2 + p
                        act.wait_ge(w_in[p], turn * 16 + 16)
                        act.wait_ge(k_cp.sem, k_cp.free(c))
                        act.activation(whi[:, p], w[:, p], ACT.Copy).then_inc(hi_done.sem, 1)
                        act.wait_ge(k_mm.sem, k_mm.done(c))
                        act.activation(kT[:, p], pk[:, :], ACT.Copy).then_inc(k_cp.sem, 1)
                        for h in range(2):
                            act.wait_ge(q_mm.sem, q_mm.done(c * 2 + h))
                            act.activation(qT[:, p, h * HALF:(h + 1) * HALF], pq[h][:, :], ACT.Copy).then_inc(q_cp.sem, 1)
                        act.wait_ge(top_done.sem, top_done.free(c))
                        for h in range(2):
                            act.wait_ge(s_mm.sem, s_mm.done(c * 2 + h))
                            act.activation(s[:, p, 4 * h:4 * h + 4], psc[h][:, :, :], ACT.Copy).then_inc(s_cp.sem, 1)

            @block.vector
            def _(dve):
                link = Chain(dve, sem("dve_route"))

                def cut_low(c, p):
                    dve.wait_ge(hi_done.sem, hi_done.done(c))
                    link(dve.tensor_tensor(wlo[:, p], w[:, p], whi[:, p].bitcast(F32), ALU.subtract), lo_done.sem)

                def search(c, p):
                    for h in range(2):
                        dve.wait_ge(s_cp.sem, s_cp.done(c * 2 + h))
                    x, y, tiles = s[:, p], s2, range(TT)
                    settle(dve, settled)
                    link.together([dve.max(tv[:, t, 0:8], x[:, t]) for t in tiles])
                    settle(dve, settled)
                    link.together([dve.max_index(tix[:, t, 0:8], tv[:, t, 0:8], x[:, t]) for t in tiles]
                                  + [dve.match_replace(y[:, t], tv[:, t, 0:8], x[:, t], NEG) for t in tiles], top_done.sem)
                    settle(dve, settled)
                    link.together([dve.max(tv[:, t, 8:16], y[:, t]) for t in tiles])
                    settle(dve, settled)
                    link.together([dve.max_index(tix[:, t, 8:16], tv[:, t, 8:16], y[:, t]) for t in tiles])
                    link(dve.tensor_copy(TV[:, :, bass.ds(c, 1), :].rearrange("p t o k -> p t (o k)"), tv[:, :, :]))
                    link(dve.tensor_copy(TI[:, :, bass.ds(c, 1), :].rearrange("p t o k -> p t (o k)"), tix[:, :, :]))

                cut_low(0, 0)
                with dve.Fori(0, HC // 2 - 1) as turn:
                    link.enter(turn, 2 * (1 + 5 * TT + 2))
                    for p in range(2):
                        cut_low(turn * 2 + (p + 1), 1 - p)
                        search(turn * 2 + p, p)
                link.leave(HC // 2 - 1)
                cut_low(HC - 1, 1)
                search(HC - 2, 0)
                search(HC - 1, 1)

            @block.tensor
            def _(pe):
                with pe.Fori(0, HC // 2) as turn:
                    for p in range(2):
                        c = turn * 2 + p
                        pe.wait_ge(k_in[p], turn * 16 + 16)
                        pe.wait_ge(k_cp.sem, k_cp.free(c))
                        pe.transpose(pk[:, :], kraw[:, p], K.ident[:, :]).then_inc(k_mm.sem, 1)
                        pe.wait_ge(lo_done.sem, lo_done.done(c))
                        for h in range(2):
                            pe.wait_ge(q_cp.sem, q_cp.free(c * 2 + h))
                            for k in range(KD):
                                last = three_pass(pe, pq[h][:, :], whi[:, p, k], wlo[:, p, k],
                                                  h2hi[:, k, h * HALF:(h + 1) * HALF], h2lo[:, k, h * HALF:(h + 1) * HALF], k, KD)
                            last.then_inc(q_mm.sem, 1)
                        for h in range(2):
                            pe.wait_ge(q_cp.sem, q_cp.done(c * 2 + h))
                            pe.wait_ge(k_cp.sem, k_cp.done(c))
                            pe.wait_ge(s_cp.sem, s_cp.free(c * 2 + h))
                            for t in range(4):
                                last = pe.matmul(psc[h][:, t], qT[:, p, (4 * h + t) * P:(4 * h + t + 1) * P], kT[:, p], start=True, stop=True)
                            last.then_inc(s_mm.sem, 1)

class Ahead:

    def __init__(self, nc, ctx, sem, keep, h2hi, h2lo, expert_u, ahead, tag, rows):
        sb = lambda n, s, d=F32: ctx.enter_context(nc.sbuf_tensor(n + tag, s, d))
        self.K, self.h2hi, self.h2lo, self.u, self.ahead = keep, h2hi, h2lo, expert_u, ahead
        self.ur, self.ge = sb("aur", [P, 2, D]), sb("age", [P, 2, HALF])
        self.uhi, self.ulo = sb("auhi", [P, 2, KD, P], F32R), sb("aulo", [P, 2, KD, P], F32R)
        self.tb, self.pa = ([ctx.enter_context(nc.psum_tensor(f"{n}{tag}{i}", [P, HALF], F32)) for i in range(2)] for n in ("atb", "apa"))
        self.u_in = [one.start(rows // 2) for one in keep.soft[0:2]]
        self.ut_mm, self.uhi_done, self.ulo_done = (Steps(sem(n + tag), 2) for n in ("aut_mm", "auhi_done", "aulo_done"))
        self.ut_rows = Steps(sem("aut_rows" + tag), 2)
        self.a_mm, self.ge_done = Steps(sem("aa_mm" + tag), 2), Steps(sem("age_done" + tag), 2)
        self.ge_out = [Steps(sem(f"age_out{tag}{h}"), 1, 16) for h in range(2)]

    def open(self, eng):
        for steps in (self.ut_mm, self.uhi_done, self.ulo_done, self.ut_rows, self.a_mm, self.ge_done, *self.ge_out):
            steps.open(eng)

    def load(self, eng, r, p, row):
        eng.wait_ge(self.ut_rows.sem, self.ut_rows.free(r))
        eng.dma_start(self.ur[:, p], self.u[bass.ds(row * P, P), :]).then_inc(self.u_in[p].sem, 16)

    def store(self, eng, r, a):
        for h in range(2):
            eng.wait_ge(self.ge_done.sem, self.ge_done.done(r * 2 + h))
            eng.dma_start(self.ahead[bass.ds(a, 1)].rearrange("o e t -> (o e) t")[:, h * HALF:(h + 1) * HALF],
                          self.ge[:, h]).then_inc(self.ge_out[h].sem, 16)

    def transpose(self, pe, r, p, at):
        pe.wait_ge(self.u_in[p].sem, self.u_in[p].value(at))
        for c in range(2):
            pe.wait_ge(self.ulo_done.sem, self.ulo_done.free(r * 2 + c))
            for k in range(4):
                last = pe.transpose(self.tb[c][:, k * P:(k + 1) * P], self.ur[:, p, (4 * c + k) * P:(4 * c + k + 1) * P], self.K.ident[:, :])
            last.then_inc(self.ut_mm.sem, 1)

    def multiply(self, pe, r, p, h, chunks):
        if chunks[0] == 0:
            if h == 0:
                pe.wait_ge(self.ulo_done.sem, self.ulo_done.done(r * 2 + 1))
            pe.wait_ge(self.ge_done.sem, self.ge_done.free(r * 2 + h))
        hs = slice(h * HALF, (h + 1) * HALF)
        for k in chunks:
            last = three_pass(pe, self.pa[h][:, :], self.uhi[:, p, k], self.ulo[:, p, k], self.h2hi[:, k, hs], self.h2lo[:, k, hs], k, KD)
        if chunks[-1] == KD - 1:
            last.then_inc(self.a_mm.sem, 1)

    def cut_high(self, act, r, p):
        for c in range(2):
            act.wait_ge(self.ut_mm.sem, self.ut_mm.done(r * 2 + c))
            act.activation(self.uhi[:, p, 4 * c:4 * c + 4], self.tb[c][:, :].rearrange("p (k e) -> p k e", k=4), ACT.Copy).then_inc(self.uhi_done.sem, 1)

    def cut_low(self, link, r, p):
        for c in range(2):
            link.eng.wait_ge(self.uhi_done.sem, self.uhi_done.done(r * 2 + c))
            link(link.eng.tensor_tensor(self.ulo[:, p, 4 * c:4 * c + 4], self.tb[c][:, :].rearrange("p (k e) -> p k e", k=4),
                                        self.uhi[:, p, 4 * c:4 * c + 4].bitcast(F32), ALU.subtract),
                 self.ulo_done.sem, *[self.ut_rows.sem] * c)

    def gelu(self, act, r, h):
        act.wait_ge(self.ge_out[h].sem, self.ge_out[h].free(r))
        act.wait_ge(self.a_mm.sem, self.a_mm.done(r * 2 + h))
        act.activation(self.ge[:, h], self.pa[h][:, :], ACT.Gelu).then_inc(self.ge_done.sem, 1)

ROWS_TILE = 4
ROWS_BLOCK = 2

PER_BEST = 1 + 5 * HEADS + 2 + 3 + 6 + 3 + 3 + 2 * ROWS_TILE

def best_phase(nc, TV, TI, iT, jT, wT, h2hi, h2lo, expert_u, ahead, keep):
    K = keep
    with ExitStack() as ctx:
        sem = ctx.enter_context(phase_semaphores(nc))
        sb = lambda n, s, d=F32: ctx.enter_context(nc.sbuf_tensor(n, s, d))
        settled = sem("b_settled")
        A = Ahead(nc, ctx, sem, K, h2hi, h2lo, expert_u, ahead, "b", TT * ROWS_TILE)
        cand = sb("cand", [P, HEADS, NBEST])
        cand2 = sb("cand2", [P, HEADS, NBEST])
        best, bj = sb("best", [P, HEADS, TOPK]), sb("bj", [P, HEADS, TOPK], U32)
        code = sb("code", [P, 2, HEADS * TOPK], U32)
        rank = sb("rank", [P, 2, HEADS * TOPK])
        eq = sb("eq", [P, HEADS, TOPK, TOPK])
        den = sb("rden", [P, HEADS])
        pick = sb("pick", [P, 3, HEADS * TOPK])
        pt = ctx.enter_context(nc.psum_tensor("rpt", [P, 3, P], F32))
        pick_done, pick_mm, pick_cp, bm_done, be_done = (sem(n) for n in ("pick_done", "pick_mm", "pick_cp", "bm_done", "be_done"))
        R = ROWS_TILE

        def row(t, j):
            return t * (4 * R // 2) + (4 * (j // 2) + j % 2)

        def turns(eng, body):
            with eng.Fori(0, TT - 1) as t:
                body(t, False)
            body(TT - 1, True)

        with nc.Block() as block:
            @block.gpsimd
            def _(pool):
                A.open(pool)
                with pool.Fori(0, TT) as t:
                    for j in range(R):
                        A.load(pool, t * R + j, j % 2, row(t, j))

            @block.sync
            def _(sp):
                with sp.Fori(0, TT) as t:
                    for j in range(R):
                        A.store(sp, t * R + j, t * R + j)
                for out in A.ge_out:
                    sp.wait_ge(out.sem, out.done(TT * R - 1))

            @block.scalar
            def _(act):
                def tile(t, last):
                    for j in range(R):
                        r = t * R + j
                        if not (last and j == R - 1):
                            A.cut_high(act, r + 1, 1 - j % 2)
                        for h in range(2):
                            A.gelu(act, r, h)
                    act.wait_ge(bm_done, t + 1)
                    act.activation(best[:, :, :], best[:, :, :], ACT.Exp).then_inc(be_done, 1)

                A.cut_high(act, 0, 0)
                turns(act, tile)

            @block.vector
            def _(dve):
                link = Chain(dve, sem("dve_best"))

                def tile(t, last):
                    def cut(j):
                        if not (last and j == R - 1):
                            A.cut_low(link, t * R + (j + 1), 1 - j % 2)

                    tl = lambda X: X[:, bass.ds(t, 1)].rearrange("p o (h c) k -> p (o h) c k", c=2)
                    va, vb = tl(TV)[:, :, 0], tl(TV)[:, :, 1]
                    link(dve.tensor_tensor(cand[:, :, :].rearrange("p h (a b) -> p h a b", b=TOPK),
                                           va[:, :, :, None].to_broadcast([P, HEADS, TOPK, TOPK]),
                                           vb[:, :, None, :].to_broadcast([P, HEADS, TOPK, TOPK]), ALU.add))
                    heads = range(HEADS)
                    settle(dve, settled)
                    link.together([dve.max(best[:, h, 0:8], cand[:, h]) for h in heads])
                    cut(0)
                    settle(dve, settled)
                    link.together([dve.max_index(bj[:, h, 0:8], best[:, h, 0:8], cand[:, h]) for h in heads]
                                  + [dve.match_replace(cand2[:, h], best[:, h, 0:8], cand[:, h], NEG) for h in heads])
                    settle(dve, settled)
                    link.together([dve.max(best[:, h, 8:16], cand2[:, h]) for h in heads])
                    cut(1)
                    settle(dve, settled)
                    link.together([dve.max_index(bj[:, h, 8:16], best[:, h, 8:16], cand2[:, h]) for h in heads])
                    link(dve.tensor_copy(den[:, :], best[:, :, 0]))
                    link(dve.tensor_tensor(best[:, :, :], best[:, :, :], den[:, :, None].to_broadcast([P, HEADS, TOPK]), ALU.subtract), bm_done)
                    bf = bj[:, :, :].rearrange("p h k -> p (h k)")
                    link(dve.tensor_single_scalar(code[:, 0], bf, 4, ALU.logical_shift_right))
                    link(dve.tensor_single_scalar(code[:, 1], bf, 15, ALU.bitwise_and))
                    link(dve.tensor_copy(rank[:, :, :], code[:, :, :]))
                    cut(2)
                    for c in range(2):
                        link(dve.tensor_tensor(eq[:, :, :, :].rearrange("p h k a -> p (h k) a"),
                                               rank[:, c, :, None].to_broadcast([P, HEADS * TOPK, TOPK]),
                                               K.iota[:, None, 0:TOPK].to_broadcast([P, HEADS * TOPK, TOPK]), ALU.is_equal))
                        link(dve.tensor_tensor(eq[:, :, :, :], eq[:, :, :, :],
                                               tl(TI)[:, :, c, None, :].to_broadcast([P, HEADS, TOPK, TOPK]), ALU.mult))
                        link(dve.tensor_reduce(pick[:, c], eq[:, :, :, :].rearrange("p h k a -> p (h k) a"), AX, ALU.add))
                    dve.wait_ge(be_done, t + 1)
                    link(dve.tensor_reduce(den[:, :], best[:, :, :], AX, ALU.add))
                    link(dve.reciprocal(den[:, :], den[:, :]))
                    link(dve.tensor_tensor(pick[:, 2].rearrange("p (h k) -> p h k", h=HEADS), best[:, :, :],
                                           den[:, :, None].to_broadcast([P, HEADS, TOPK]), ALU.mult), pick_done)
                    cut(3)
                    dve.wait_ge(pick_mm, t + 1)
                    for c, dst in enumerate((iT, jT, wT)):
                        link(dve.tensor_copy(dst[:, bass.ds(t * P, P)], pt[:, c]), *[pick_cp] * (c == 2))

                A.cut_low(link, 0, 0)
                with dve.Fori(0, TT - 1) as t:
                    link.enter(t, PER_BEST)
                    tile(t, False)
                link.leave(TT - 1)
                tile(TT - 1, True)

            @block.tensor
            def _(pe):
                def tile(t, last):
                    for j in range(R):
                        r, p = t * R + j, j % 2
                        if not (last and j == R - 1):
                            A.transpose(pe, r + 1, 1 - p, (t * (R // 2) + (j + 1) // 2) * 16 + 16)
                        for h in range(2):
                            A.multiply(pe, r, p, h, range(KD))
                    pe.wait_ge(pick_done, t + 1)
                    for c in range(3):
                        step = pe.transpose(pt[:, c], pick[:, c], K.ident[:, :])
                    step.then_inc(pick_mm, 1)

                A.transpose(pe, 0, 0, 16)
                turns(pe, tile)

def gate_phase(nc, iT, jT, wT, gates, h2hi, h2lo, expert_u, ahead, keep):
    K = keep
    BT = 64
    G = 4
    NG = BT // G
    PER = NG // ROWS_BLOCK
    CH = 2 * KD // PER
    NB = T // BT
    A0 = TT * ROWS_TILE
    R0 = 2 * A0
    with ExitStack() as ctx:
        sem = ctx.enter_context(phase_semaphores(nc))
        sb = lambda n, s, d=F32: ctx.enter_context(nc.sbuf_tensor(n, s, d))
        A = Ahead(nc, ctx, sem, K, h2hi, h2lo, expert_u, ahead, "g", NB * ROWS_BLOCK)
        col = sb("gcol", [P, 2 * G, P])
        row = sb("grow", [P, 2 * G, P])
        stage = sb("gstage", [P, P, 2 * BT])
        pg = [ctx.enter_context(nc.psum_tensor(f"gp{i}", [P, G, P], F32)) for i in range(2)]
        hot_done, g_mm, g_cp = Steps(sem("hot_done"), 2), Steps(sem("g_mm"), 2), Steps(sem("g_cp"), 2)
        st_out = [Steps(sem(f"st_out{i}"), 1, 16) for i in range(2)]
        gv = gates.rearrange("i j t -> j i t")

        def turns(eng, body):
            with eng.Fori(0, NB // 2 - 1) as turn:
                body(turn, False)
            body(NB // 2 - 1, True)

        with nc.Block() as block:
            @block.gpsimd
            def _(pool):
                A.open(pool)
                for steps in (hot_done, g_mm, g_cp, *st_out):
                    steps.open(pool)
                with pool.Fori(0, NB) as b:
                    for j in range(ROWS_BLOCK):
                        A.load(pool, b * 2 + j, j, b * 4 + (R0 + j))

            @block.vector
            def _(dve):
                link = Chain(dve, sem("dve_gate"))

                def body(turn, last):
                    for half in range(2):
                        b = turn * 2 + half
                        for gi in range(NG):
                            u = gi % 2
                            dve.wait_ge(g_mm.sem, g_mm.free(b * NG + gi))
                            for q in range(G):
                                at = bass.ds(b * BT + (gi * G + q), 1)
                                dve.tensor_scalar(col[:, u * G + q], K.iota[:, :], jT[:, at], None, ALU.is_equal)
                                step = dve.tensor_scalar(row[:, u * G + q], K.iota[:, :], iT[:, at], wT[:, at], ALU.is_equal, ALU.mult)
                            step.then_inc(hot_done.sem, 1)
                            j, k = divmod(gi, PER)
                            if k == 5 and not (last and half == 1 and j == ROWS_BLOCK - 1):
                                A.cut_low(link, b * 2 + (j + 1), 1 - j)

                A.cut_low(link, 0, 0)
                with dve.Fori(0, NB // 2 - 1) as turn:
                    link.enter(turn, 2 * 2 * ROWS_BLOCK)
                    body(turn, False)
                link.leave(NB // 2 - 1)
                body(NB // 2 - 1, True)

            @block.tensor
            def _(pe):
                def body(turn, last):
                    for half in range(2):
                        b = turn * 2 + half
                        for gi in range(NG):
                            u = gi % 2
                            pe.wait_ge(hot_done.sem, hot_done.done(b * NG + gi))
                            pe.wait_ge(g_cp.sem, g_cp.free(b * NG + gi))
                            for q in range(G):
                                step = pe.matmul(pg[u][:, q], col[:, u * G + q], row[:, u * G + q], start=True, stop=True)
                            step.then_inc(g_mm.sem, 1)
                            j, k = divmod(gi, PER)
                            h, c = divmod(k * CH, KD)
                            A.multiply(pe, b * 2 + j, j, h, range(c, c + CH))
                            if k == 3 and not (last and half == 1 and j == ROWS_BLOCK - 1):
                                A.transpose(pe, b * 2 + (j + 1), 1 - j, (b + j) * 16 + 16)

                A.transpose(pe, 0, 0, 16)
                turns(pe, body)

            @block.scalar
            def _(act):
                def body(turn, last):
                    for half in range(2):
                        b = turn * 2 + half
                        act.wait_ge(st_out[half].sem, st_out[half].free(turn))
                        for gi in range(NG):
                            at = half * BT + gi * G
                            act.wait_ge(g_mm.sem, g_mm.done(b * NG + gi))
                            act.activation(stage[:, :, at:at + G].rearrange("p i t -> p t i"), pg[gi % 2][:, :, :], ACT.Copy).then_inc(g_cp.sem, 1)
                            j, k = divmod(gi, PER)
                            if k == 4:
                                A.gelu(act, b * 2 + j, 0)
                                if not (last and half == 1 and j == ROWS_BLOCK - 1):
                                    A.cut_high(act, b * 2 + (j + 1), 1 - j)
                            if k == 0 and gi:
                                A.gelu(act, b * 2 + (j - 1), 1)
                        A.gelu(act, b * 2 + (ROWS_BLOCK - 1), 1)

                A.cut_high(act, 0, 0)
                turns(act, body)

            @block.sync
            def _(sp):
                with sp.Fori(0, NB // 2) as turn:
                    for half in range(2):
                        b = turn * 2 + half
                        for j in range(ROWS_BLOCK):
                            A.store(sp, b * 2 + j, b * 2 + (A0 + j))
                        sp.wait_ge(g_cp.sem, g_cp.done(b * NG + (NG - 1)))
                        sp.dma_start(gv[:, :, bass.ds(b * BT, BT)],
                                     stage[:, :, half * BT:(half + 1) * BT]).then_inc(st_out[half].sem, 16)
                for half in range(2):
                    sp.wait_ge(st_out[half].sem, st_out[half].done(NB // 2 - 1))
                for out in A.ge_out:
                    sp.wait_ge(out.sem, out.done(NB * ROWS_BLOCK - 1))

def expert_phase(nc, h2hi, h2lo, expert_u, expert_v, gates, ahead, acc, keep):
    K = keep
    Q = 4
    GROUPS = NKEYS // Q
    ORDER = (0, 2, 1, 3)
    with ExitStack() as ctx:
        sem = ctx.enter_context(phase_semaphores(nc))
        sb = lambda n, s, d=F32: ctx.enter_context(nc.sbuf_tensor(n, s, d))
        ur, vr, gr = sb("ur", [P, D]), sb("vraw", [P, 2, D]), sb("gr", [P, 2, T])
        uhi, ulo = sb("uhi", [P, 2, KD, P], F32R), sb("ulo", [P, 2, KD, P], F32R)
        vhi, vlo = sb("vhi", [P, Q, D], F32R), sb("vlo", [P, Q, D], F32R)
        Hhi, Hlo = sb("Hhi", [P, Q, T], F32R), sb("Hlo", [P, Q, T], F32R)
        ge = sb("ge", [P, 2, HALF])
        ga = sb("ga", [P, T])
        tb, pa = ([ctx.enter_context(nc.psum_tensor(f"{n}{i}", [P, HALF], F32)) for i in range(2)] for n in ("etb", "epa"))
        vo = [ctx.enter_context(nc.psum_tensor(f"evo{i}", [P, HALF], F32)) for i in range(4)]
        u_in, v_in = sem("u_in"), [sem(f"v_in{i}") for i in range(2)]
        g_in, ga_in = [one.start(2 * GROUPS) for one in keep.soft[0:2]], keep.soft[2].start(2 * GROUPS)
        ut_mm, uhi_done, ulo_done, a_mm, ge_done = (Steps(sem(n), 2) for n in ("ut_mm", "uhi_done", "ulo_done", "a_mm", "ge_done"))
        ut_rows = Steps(sem("ut_rows"), 1)
        ga_free = Steps(sem("ga_free"), 1)
        vhi_done, vlo_done = Steps(sem("vhi_done"), 2), Steps(sem("vlo_done"), 2)
        H_done, Hhi_done, Hlo_done = (Steps(sem(n), 2) for n in ("H_done", "Hhi_done", "Hlo_done"))
        g_free = Steps(sem("g_free"), 2)
        vo_mm, vo_add = Steps(sem("vo_mm"), 4), Steps(sem("vo_add"), 4)
        UNITS = 2 * TT

        def turns(eng, body, link=None, per=0):
            with eng.Fori(0, GROUPS - 1) as g:
                if link:
                    link.enter(g, per)
                body(g, False)
            if link:
                link.leave(GROUPS - 1)
            body(GROUPS - 1, True)

        with nc.Block() as block:
            @block.sync
            def _(sp):
                for steps in (ut_mm, ut_rows, uhi_done, ulo_done, vhi_done, vlo_done, a_mm, ge_done, H_done, Hhi_done, Hlo_done,
                              g_free, ga_free, vo_mm, vo_add):
                    steps.open(sp)

                def load_u(g, p):
                    sp.wait_ge(ut_rows.sem, ut_rows.free(g * 2 + p))
                    sp.dma_start(ur[:, :], expert_u[bass.ds(g * (Q * P) + (2 + p) * P, P), :]).then_inc(u_in, 16)

                def group(g, last):
                    for i, q in enumerate(ORDER):
                        sp.wait_ge(vlo_done.sem, vlo_done.free(g * Q + i))
                        sp.dma_start(vr[:, i % 2], expert_v[bass.ds(g * (Q * P) + q * P, P), :]).then_inc(v_in[i % 2], 16)
                        if i % 2 and not last:
                            load_u(g + 1, i // 2)

                load_u(0, 0)
                load_u(0, 1)
                turns(sp, group)

            @block.gpsimd
            def _(pool):
                with pool.Fori(0, GROUPS) as g:
                    for i, q in enumerate(ORDER):
                        if q < 2:
                            pool.wait_ge(ga_free.sem, ga_free.free(g * 2 + q))
                            pool.dma_start(ga[:, :], ahead[bass.ds(g * 2 + q, 1)].rearrange("o e t -> (o e) t")).then_inc(ga_in.sem, 16)
                        pool.wait_ge(g_free.sem, g_free.free(g * Q + i))
                        pool.dma_start(gr[:, i % 2], gates[bass.ds(g * Q + q, 1)].rearrange("o j t -> (o j) t")).then_inc(g_in[i % 2].sem, 16)

            @block.scalar
            def _(act):
                link = Chain(act, sem("act_experts"))

                def cut_u(m, p):
                    for c in range(2):
                        act.wait_ge(ut_mm.sem, ut_mm.done(m * 2 + c))
                        link(act.activation(uhi[:, p, 4 * c:4 * c + 4], tb[c][:, :].rearrange("p (k e) -> p k e", k=4), ACT.Copy), uhi_done.sem)

                def cut_v(g, i):
                    act.wait_ge(v_in[i % 2], (g * 32 + (i // 2) * 16) + 16)
                    act.wait_ge(vo_mm.sem, vo_mm.free(g * UNITS + 3))
                    link(act.activation(vhi[:, ORDER[i]], vr[:, i % 2], ACT.Copy), vhi_done.sem)

                def row(g, i):
                    q, n = ORDER[i], g * Q + i
                    for h in range(2):
                        hs = slice(h * HALF, (h + 1) * HALF)
                        if q >= 2:
                            act.wait_ge(a_mm.sem, a_mm.done((g * 2 + (q - 2)) * 2 + h))
                            link(act.activation(ge[:, h], pa[h][:, :], ACT.Gelu), ge_done.sem)
                        act.wait_ge(H_done.sem, H_done.done(n * 2 + h))
                        link(act.activation(Hhi[:, q, hs], gr[:, i % 2, hs], ACT.Copy), Hhi_done.sem)

                def group(g, last):
                    cut_u(g * 2 + 1, 1)
                    cut_v(g, 0)
                    row(g, 0)
                    cut_v(g, 1)
                    cut_v(g, 2)
                    row(g, 1)
                    row(g, 2)
                    cut_v(g, 3)
                    row(g, 3)
                    if not last:
                        cut_u(g * 2 + 2, 0)

                cut_u(0, 0)
                turns(act, group, link, 2 * 2 + Q + 2 * 2 + 2 * Q)

            @block.vector
            def _(dve):
                link = Chain(dve, sem("dve_experts"))

                def cut_u(m, p):
                    for c in range(2):
                        dve.wait_ge(uhi_done.sem, uhi_done.done(m * 2 + c))
                        link(dve.tensor_tensor(ulo[:, p, 4 * c:4 * c + 4], tb[c][:, :].rearrange("p (k e) -> p k e", k=4),
                                               uhi[:, p, 4 * c:4 * c + 4].bitcast(F32), ALU.subtract), ulo_done.sem, *[ut_rows.sem] * c)

                def cut_v(g, i):
                    dve.wait_ge(vhi_done.sem, vhi_done.done(g * Q + i))
                    link(dve.tensor_tensor(vlo[:, ORDER[i]], vr[:, i % 2], vhi[:, ORDER[i]].bitcast(F32), ALU.subtract), vlo_done.sem)

                def row(g, i):
                    q, n = ORDER[i], g * Q + i
                    dve.wait_ge(g_in[i % 2].sem, g_in[i % 2].value((g * 32 + (i // 2) * 16) + 16))
                    if q < 2:
                        dve.wait_ge(ga_in.sem, ga_in.value((g * 32 + q * 16) + 16))
                    def gate(h):
                        hs = slice(h * HALF, (h + 1) * HALF)
                        if q >= 2:
                            dve.wait_ge(ge_done.sem, ge_done.done((g * 2 + (q - 2)) * 2 + h))
                        src, free = (ge[:, h], ()) if q >= 2 else (ga[:, hs], [ga_free.sem] * h)
                        link(dve.tensor_tensor(gr[:, i % 2, hs], gr[:, i % 2, hs], src, ALU.mult), H_done.sem, *free)

                    def cut_low(h):
                        hs = slice(h * HALF, (h + 1) * HALF)
                        dve.wait_ge(Hhi_done.sem, Hhi_done.done(n * 2 + h))
                        link(dve.tensor_tensor(Hlo[:, q, hs], gr[:, i % 2, hs], Hhi[:, q, hs].bitcast(F32), ALU.subtract),
                             Hlo_done.sem, *[g_free.sem] * h)

                    for step, h in ((gate, 0), (gate, 1), (cut_low, 0), (cut_low, 1)) if q < 2 else ((gate, 0), (cut_low, 0), (gate, 1), (cut_low, 1)):
                        step(h)

                def group(g, last):
                    cut_u(g * 2 + 1, 1)
                    cut_v(g, 0)
                    row(g, 0)
                    cut_v(g, 1)
                    cut_v(g, 2)
                    row(g, 1)
                    row(g, 2)
                    cut_v(g, 3)
                    row(g, 3)
                    if not last:
                        cut_u(g * 2 + 2, 0)
                    for u in range(UNITS):
                        dve.wait_ge(vo_mm.sem, vo_mm.done(g * UNITS + u))
                        at = acc[:, u // 2, (u % 2) * HALF:(u % 2 + 1) * HALF]
                        link(dve.tensor_tensor(at, at, vo[u % 4][:, :], ALU.add), vo_add.sem)

                link(dve.memset(acc[:, :, :], 0.0))
                cut_u(0, 0)
                turns(dve, group, link, 2 * 2 + Q * 5 + UNITS)

            @block.tensor
            def _(pe):
                def turn_u(m):
                    pe.wait_ge(u_in, m * 16 + 16)
                    for c in range(2):
                        pe.wait_ge(ulo_done.sem, ulo_done.free(m * 2 + c))
                        for k in range(4):
                            step = pe.transpose(tb[c][:, k * P:(k + 1) * P], ur[:, (4 * c + k) * P:(4 * c + k + 1) * P], K.ident[:, :])
                        step.then_inc(ut_mm.sem, 1)

                def group(g, last):
                    for p in range(2):
                        m = g * 2 + p
                        if not (last and p):
                            turn_u(m + 1)
                        pe.wait_ge(ulo_done.sem, ulo_done.done(m * 2 + 1))
                        for h in range(2):
                            pe.wait_ge(ge_done.sem, ge_done.free(m * 2 + h))
                            for k in range(KD):
                                step = three_pass(pe, pa[h][:, :], uhi[:, p, k], ulo[:, p, k], h2hi[:, k, h * HALF:(h + 1) * HALF],
                                                  h2lo[:, k, h * HALF:(h + 1) * HALF], k, KD)
                            step.then_inc(a_mm.sem, 1)
                    for u in range(UNITS):
                        t, dh = u // 2, u % 2
                        if u in (0, UNITS // 2):
                            pe.wait_ge(Hlo_done.sem, Hlo_done.done((g * Q + (Q - 1)) * 2 + u // (UNITS // 2)))
                        pe.wait_ge(vo_add.sem, vo_add.free(g * UNITS + u))
                        for q in range(Q):
                            step = three_pass(pe, vo[u % 4][:, :], Hhi[:, q, t * P:(t + 1) * P], Hlo[:, q, t * P:(t + 1) * P],
                                              vhi[:, q, dh * HALF:(dh + 1) * HALF], vlo[:, q, dh * HALF:(dh + 1) * HALF], q, Q)
                        step.then_inc(vo_mm.sem, 1)

                turn_u(0)
                turns(pe, group)

def finish_phase(nc, acc, x1, gate2_dram, out, keep):
    with ExitStack() as ctx:
        sem = ctx.enter_context(phase_semaphores(nc))
        sb = lambda n, s, d=F32: ctx.enter_context(nc.sbuf_tensor(n, s, d))
        gate = sb("gate2", [P, D])
        xt = sb("fx", [P, TT, D])
        gate_in, f_in, f_done, f_out = sem("gate_in"), [sem(f"f_in{t}") for t in range(TT)], sem("f_done"), sem("f_out")
        with nc.Block() as block:
            @block.sync
            def _(sp):
                sp.dma_start(gate[:, :], gate2_dram.to_broadcast([P, D])).then_inc(gate_in, 16)
                for t in range(TT):
                    sp.dma_start(xt[:, t], x1[t * P:(t + 1) * P, :]).then_inc(f_in[t], 16)
                for t in range(TT):
                    sp.wait_ge(f_done, t + 1)
                    sp.dma_start(out[t * P:(t + 1) * P, :], xt[:, t]).then_inc(f_out, 16)
                sp.wait_ge(f_out, 16 * TT)

            @block.vector
            def _(dve):
                link = Chain(dve, sem("dve_finish"))
                dve.wait_ge(gate_in, 16)
                for t in range(TT):
                    link(dve.tensor_tensor(acc[:, t], acc[:, t], gate[:, :], ALU.mult))
                    dve.wait_ge(f_in[t], 16)
                    link(dve.tensor_tensor(xt[:, t], xt[:, t], acc[:, t], ALU.add), f_done)

class Keep:
    pass

def program(nc, io, out):
    dram = lambda n, s: nc.dram_tensor(n, s, F32, kind="Internal").ap()
    io["mod_dram"] = dram("mod_dram", [N_MOD * D])
    proj = dram("proj_dram", [T, D_IN])
    x1 = dram("x1_dram", [T, D])
    ahead = dram("ahead_dram", [NKEYS // 2, NKEYS, T])
    gates = dram("gates_dram", [NKEYS, NKEYS, T])
    K = Keep()
    with ExitStack() as ctx:
        sb = lambda n, s, d=F32: ctx.enter_context(nc.sbuf_tensor(n, s, d))
        K.ident = sb("ident", [P, P])
        K.soft = [Soft(ctx.enter_context(nc.semaphore(f"soft_dma{i}"))) for i in range(4)]
        K.iota = sb("iota", [P, P])
        K.par = sb("par", [P, 32])
        K.mod = sb("mod", [P, 6 * KD])
        K.a1, K.a2 = sb("a1", [P, KD]), sb("a2", [P, KD])
        K.lbd, K.lbs = sb("lbd", [P, NH]), sb("lbs", [P, NH])
        K.eps = sb("eps", [P, 1])
        K.hgw, K.qw, K.kw, K.sink = sb("hgw", [P, P]), sb("qw", [P, HD]), sb("kw", [P, HD]), sb("sink", [P, SWH])
        setup_phase(nc, io, K)
        with ExitStack() as c2:
            hhi = c2.enter_context(nc.sbuf_tensor("hhi", [P, KD, T], F32R))
            hlo = c2.enter_context(nc.sbuf_tensor("hlo", [P, KD, T], F32R))
            norm_phase(nc, "1", io["x"][0], K.a1, K.mod[:, 0:8], hhi, hlo, K)
            W = D_IN // 16
            token_gemm_phase(nc, "i", hhi, hlo, KD, io["w_in"][0].rearrange("(k p) n -> p k n", p=P), W, 16, proj, K)
        with ExitStack() as c2:
            yhi = c2.enter_context(nc.sbuf_tensor("yhi", [P, KD, T], F32R))
            ylo = c2.enter_context(nc.sbuf_tensor("ylo", [P, KD, T], F32R))
            mixer_phase(nc, proj, yhi, ylo, K)
            merge_phase(nc, yhi, ylo, proj, io["w_branch"], io["w_out"], io["x"][0],
                        io["mod_dram"][None, 2 * D:3 * D], x1, K)
        h2hi, h2lo = sb("h2hi", [P, KD, T], F32R), sb("h2lo", [P, KD, T], F32R)
        norm_phase(nc, "2", x1, K.a2, K.mod[:, 24:32], h2hi, h2lo, K)
        with ExitStack() as c2:
            iT, jT, wT = (c2.enter_context(nc.sbuf_tensor(n, [P, T], F32)) for n in ("iT", "jT", "wT"))
            with ExitStack() as c3:
                TV, TI = (c3.enter_context(nc.sbuf_tensor(n, [P, TT, HC, TOPK], F32)) for n in ("TV", "TI"))
                route_phase(nc, h2hi, h2lo, io["w_query"][0], io["sub_keys"][0], TV, TI, K)
                best_phase(nc, TV, TI, iT, jT, wT, h2hi, h2lo, io["expert_u"][0], ahead, K)
            gate_phase(nc, iT, jT, wT, gates, h2hi, h2lo, io["expert_u"][0], ahead, K)
        acc = sb("acc", [P, TT, D])
        expert_phase(nc, h2hi, h2lo, io["expert_u"][0], io["expert_v"][0], gates, ahead, acc, K)
        finish_phase(nc, acc, x1, io["mod_dram"][None, 5 * D:6 * D], out[0], K)

_INS = ["x", "c", "w_ada", "b_ada", "norm_mix_w", "w_in", "hg_lb_raw", "hg_norm_w", "q_norm_w", "k_norm_w", "sinks",
        "w_branch", "w_out", "norm_ffn_w", "w_query", "sub_keys", "expert_u", "expert_v"]

def kernel(**inputs):
    import concourse.bacc as _bacc
    from concourse.bass_utils import run_bass_kernel_spmd as _run

    nc = _bacc.Bacc("TRN2", target_bir_lowering=False, num_devices=1)
    arrays, io = {}, {}
    for name in _INS:
        a = np.ascontiguousarray(inputs[name])
        arrays[f"in_{name}"] = a
        io[name] = nc.dram_tensor(f"in_{name}", a.shape, mybir.dt.from_np(a.dtype), kind="ExternalInput").ap()
    out = nc.dram_tensor("out_0", (1, T, D), F32, kind="ExternalOutput").ap()
    program(nc, io, out)
    r = _run(nc, [arrays], core_ids=[0])
    return r.results[0]["out_0"]
```
